# Optimizing a Trainium2 kernel written in Bass

```python
import math
import jax, jax.numpy as jnp
from jax import lax
import numpy as np
import jax
import jax.numpy as jnp

D_MODEL = 1024
BATCH = 1
SEQ = 256
DEPTH = 2

SGU_CHUNK = 128
SGU_GROUPS = 4
SGU_WIDTH = 512
SGU_GROUP_W = SGU_WIDTH // SGU_GROUPS
SSM_WIDTH = 512
SSM_GROUP = 16
SSM_GROUPS = SSM_WIDTH // SSM_GROUP
SSM_STATE = 64
DT_MIN = 0.001
DT_MAX = 0.1
ATT_HEADS = 8
HEAD_DIM = 64
ATT_WIDTH = ATT_HEADS * HEAD_DIM
MOBA_BLOCK = 256
MOBA_TOPK = 3
Q_CHUNK = 128
N_BRANCH = 3
IN_COLS = 2 * SGU_WIDTH + SSM_WIDTH + 3 * ATT_WIDTH + N_BRANCH * D_MODEL
D_FF = -(-8 * D_MODEL // (3 * 256)) * 256
DN_ALPHA = (2 * DEPTH) ** 0.25
DN_BETA = (8 * DEPTH) ** -0.25
LN_EPS = 1e-5
NEG_INF = -1e30


def layer_norm(x, g, b):
    xf = x.astype(jnp.float32)
    mu = jnp.mean(xf, axis=-1, keepdims=True)
    var = jnp.mean(jnp.square(xf - mu), axis=-1, keepdims=True)
    return ((xf - mu) * lax.rsqrt(var + LN_EPS) * g.astype(jnp.float32) + b.astype(jnp.float32)).astype(x.dtype)

def spatial_gating(z, ln_g, ln_b, w_s, b_s):
    u, v = jnp.split(z, 2, axis=-1)
    v = layer_norm(v, ln_g, ln_b)
    bn, s, _ = v.shape
    v = v.reshape(bn, s // SGU_CHUNK, SGU_CHUNK, SGU_GROUPS, SGU_GROUP_W)
    w = jnp.tril(w_s)
    mixed = jnp.einsum('gts,bnsgc->bntgc', w, v) + b_s.T[:, :, None]
    return u * mixed.reshape(bn, s, SGU_WIDTH)

def s5_branch(u, lam_re, lam_im, log_dt, b_re, b_im, c_re, c_im, d, glu_w, glu_b):
    f32 = jnp.float32
    bn, s, _ = u.shape
    lam = lax.complex(lam_re.astype(f32), lam_im.astype(f32))
    dt = jnp.exp(log_dt.astype(f32))[:, None]
    lam_bar = jnp.exp(lam * dt)
    b_mat = lax.complex(b_re.astype(f32), b_im.astype(f32))
    b_bar = ((lam_bar - 1.0) / lam)[..., None] * b_mat
    uf = u.astype(f32)
    ug = uf.reshape(bn, s, SSM_GROUPS, SSM_GROUP).astype(jnp.complex64)
    bu = jnp.einsum('gph,bsgh->bsgp', b_bar, ug)
    a = jnp.broadcast_to(lam_bar, bu.shape)

    def combine(left, right):
        a_l, b_l = left
        a_r, b_r = right
        return a_r * a_l, a_r * b_l + b_r

    _, h = lax.associative_scan(combine, (a, bu), axis=1)
    c_mat = lax.complex(c_re.astype(f32), c_im.astype(f32))
    y = jnp.real(jnp.einsum('ghp,bsgp->bsgh', c_mat, h)).reshape(bn, s, SSM_WIDTH)
    y = jax.nn.gelu(y + d.astype(f32) * uf)
    y = y * jax.nn.sigmoid(y @ glu_w.astype(f32) + glu_b.astype(f32))
    return y.astype(u.dtype)

def moba_attention(q, k, v):
    f32 = jnp.float32
    bn, s = q.shape[0], q.shape[1]
    s_pad = -(-s // MOBA_BLOCK) * MOBA_BLOCK
    pad = ((0, 0), (0, s_pad - s), (0, 0), (0, 0))
    q = jnp.pad(q, pad).transpose(0, 2, 1, 3)
    k = jnp.pad(k, pad).transpose(0, 2, 1, 3)
    v = jnp.pad(v, pad).transpose(0, 2, 1, 3)
    nb = s_pad // MOBA_BLOCK
    n_sel = min(MOBA_TOPK, nb)
    kb = k.reshape(bn, ATT_HEADS, nb, MOBA_BLOCK, HEAD_DIM)
    vb = v.reshape(bn, ATT_HEADS, nb, MOBA_BLOCK, HEAD_DIM)
    k_mean = jnp.mean(kb.astype(f32), axis=3)
    pos = jnp.arange(s_pad, dtype=jnp.int32)
    q_blk = pos // MOBA_BLOCK
    gate = jnp.einsum('bhsd,bhnd->bhsn', q.astype(f32), k_mean)
    fully_past = jnp.arange(nb, dtype=jnp.int32)[None, :] < q_blk[:, None]
    gate = jnp.where(fully_past, gate, -jnp.inf)
    _, sel = lax.top_k(gate, n_sel)
    kb_flat = kb.reshape(bn * ATT_HEADS * nb, MOBA_BLOCK, HEAD_DIM)
    vb_flat = vb.reshape(bn * ATT_HEADS * nb, MOBA_BLOCK, HEAD_DIM)
    bh_off = (jnp.arange(bn * ATT_HEADS, dtype=jnp.int32) * nb).reshape(bn, ATT_HEADS, 1, 1)
    slopes = 2.0 ** (-8.0 * jnp.arange(1, ATT_HEADS + 1, dtype=f32) / ATT_HEADS)
    scale = HEAD_DIM ** -0.5
    n_chunks = s_pad // Q_CHUNK
    qc = q.reshape(bn, ATT_HEADS, n_chunks, Q_CHUNK, HEAD_DIM).transpose(2, 0, 1, 3, 4)
    selc = sel.reshape(bn, ATT_HEADS, n_chunks, Q_CHUNK, n_sel).transpose(2, 0, 1, 3, 4)
    chunk_ids = jnp.arange(n_chunks, dtype=jnp.int32)
    blk_ar = jnp.arange(MOBA_BLOCK, dtype=jnp.int32)

    def body(args):
        c, q_c, sel_c = args
        t = c * Q_CHUNK + jnp.arange(Q_CHUNK, dtype=jnp.int32)
        own = (c * Q_CHUNK) // MOBA_BLOCK
        kg = kb_flat[sel_c + bh_off]
        vg = vb_flat[sel_c + bh_off]
        s_g = jnp.einsum('bhqd,bhqkld->bhqkl', q_c, kg, preferred_element_type=f32) * scale
        key_pos_g = sel_c[..., None] * MOBA_BLOCK + blk_ar
        dist_g = jnp.abs(t[:, None, None] - key_pos_g).astype(f32)
        valid_g = jnp.arange(n_sel, dtype=jnp.int32)[None, :] < (t // MOBA_BLOCK)[:, None]
        s_g = jnp.where(valid_g[None, None, :, :, None], s_g - slopes[None, :, None, None, None] * dist_g, NEG_INF)
        k_own = lax.dynamic_index_in_dim(kb, own, axis=2, keepdims=False)
        v_own = lax.dynamic_index_in_dim(vb, own, axis=2, keepdims=False)
        s_o = jnp.einsum('bhqd,bhld->bhql', q_c, k_own, preferred_element_type=f32) * scale
        dist_o = t[:, None] - (own * MOBA_BLOCK + blk_ar)[None, :]
        s_o = jnp.where((dist_o >= 0)[None, None], s_o - slopes[None, :, None, None] * jnp.abs(dist_o).astype(f32), NEG_INF)
        scores = jnp.concatenate([s_g.reshape(bn, ATT_HEADS, Q_CHUNK, n_sel * MOBA_BLOCK), s_o], axis=-1)
        p = jax.nn.softmax(scores, axis=-1).astype(v.dtype)
        p_g = p[..., : n_sel * MOBA_BLOCK].reshape(bn, ATT_HEADS, Q_CHUNK, n_sel, MOBA_BLOCK)
        p_o = p[..., n_sel * MOBA_BLOCK:]
        out = (jnp.einsum('bhqkl,bhqkld->bhqd', p_g, vg, preferred_element_type=f32)
               + jnp.einsum('bhql,bhld->bhqd', p_o, v_own, preferred_element_type=f32))
        return out.astype(v.dtype)

    o = lax.map(body, (chunk_ids, qc, selc))
    o = o.transpose(1, 0, 3, 2, 4).reshape(bn, s_pad, ATT_WIDTH)
    return o[:, :s]

def hybrid_mixer(x, w_in, sgu_ln_g, sgu_ln_b, sgu_w, sgu_b, lam_re, lam_im, log_dt, b_re, b_im,
                 c_re, c_im, d, glu_w, glu_b, w_a, w_b, w_c, w_out):
    bn, s, _ = x.shape
    proj = x @ w_in
    splits = np.cumsum([2 * SGU_WIDTH, SSM_WIDTH, ATT_WIDTH, ATT_WIDTH, ATT_WIDTH]).tolist()
    z_sgu, z_ssm, q, k, v, gates = jnp.split(proj, splits, axis=-1)
    br_a = spatial_gating(jax.nn.gelu(z_sgu), sgu_ln_g, sgu_ln_b, sgu_w, sgu_b)
    br_b = s5_branch(z_ssm, lam_re, lam_im, log_dt, b_re, b_im, c_re, c_im, d, glu_w, glu_b)
    hd = (bn, s, ATT_HEADS, HEAD_DIM)
    br_c = moba_attention(q.reshape(hd), k.reshape(hd), v.reshape(hd))
    g = jax.nn.sigmoid(gates.astype(jnp.float32)).astype(x.dtype).reshape(bn, s, N_BRANCH, D_MODEL)
    merged = g[:, :, 0] * (br_a @ w_a) + g[:, :, 1] * (br_b @ w_b) + g[:, :, 2] * (br_c @ w_c)
    return merged @ w_out

def swiglu(x, w1, w3, w2):
    return (jax.nn.silu(x @ w1) * (x @ w3)) @ w2

def first_inputs(seed: int = 0) -> dict:
    key = jax.random.key(seed)
    ks = jax.random.split(key, 32)
    L = DEPTH
    nrm = lambda k, shape, sc: jax.random.normal(k, shape, jnp.float32) * sc
    lam_im0 = jnp.pi * jnp.arange(SSM_STATE, dtype=jnp.float32)
    return {
        "x": nrm(ks[0], (BATCH, SEQ, D_MODEL), 1.0),
        "w_in": nrm(ks[1], (L, D_MODEL, IN_COLS), D_MODEL ** -0.5),
        "sgu_ln_g": 1.0 + nrm(ks[2], (L, SGU_WIDTH), 0.02),
        "sgu_ln_b": nrm(ks[3], (L, SGU_WIDTH), 0.02),
        "sgu_w": nrm(ks[4], (L, SGU_GROUPS, SGU_CHUNK, SGU_CHUNK), SGU_CHUNK ** -0.5),
        "sgu_b": 1.0 + nrm(ks[5], (L, SGU_GROUPS, SGU_CHUNK), 0.02),
        "ssm_lambda_re": -0.5 + nrm(ks[6], (L, SSM_GROUPS, SSM_STATE), 0.01),
        "ssm_lambda_im": lam_im0 + nrm(ks[7], (L, SSM_GROUPS, SSM_STATE), 0.01),
        "ssm_log_dt": jax.random.uniform(ks[8], (L, SSM_GROUPS), jnp.float32, math.log(DT_MIN), math.log(DT_MAX)),
        "ssm_b_re": nrm(ks[9], (L, SSM_GROUPS, SSM_STATE, SSM_GROUP), (2 * SSM_GROUP) ** -0.5),
        "ssm_b_im": nrm(ks[10], (L, SSM_GROUPS, SSM_STATE, SSM_GROUP), (2 * SSM_GROUP) ** -0.5),
        "ssm_c_re": nrm(ks[11], (L, SSM_GROUPS, SSM_GROUP, SSM_STATE), (2 * SSM_STATE) ** -0.5),
        "ssm_c_im": nrm(ks[12], (L, SSM_GROUPS, SSM_GROUP, SSM_STATE), (2 * SSM_STATE) ** -0.5),
        "ssm_d": nrm(ks[13], (L, SSM_WIDTH), 1.0),
        "glu_w": nrm(ks[14], (L, SSM_WIDTH, SSM_WIDTH), SSM_WIDTH ** -0.5),
        "glu_b": nrm(ks[15], (L, SSM_WIDTH), 0.02),
        "w_branch_a": nrm(ks[16], (L, SGU_WIDTH, D_MODEL), SGU_WIDTH ** -0.5),
        "w_branch_b": nrm(ks[17], (L, SSM_WIDTH, D_MODEL), SSM_WIDTH ** -0.5),
        "w_branch_c": nrm(ks[18], (L, ATT_WIDTH, D_MODEL), ATT_WIDTH ** -0.5),
        "w_out": nrm(ks[19], (L, D_MODEL, D_MODEL), DN_BETA * D_MODEL ** -0.5),
        "ln1_g": 1.0 + nrm(ks[20], (L, D_MODEL), 0.02),
        "ln1_b": nrm(ks[21], (L, D_MODEL), 0.02),
        "ffn_w1": nrm(ks[22], (L, D_MODEL, D_FF), D_MODEL ** -0.5),
        "ffn_w3": nrm(ks[23], (L, D_MODEL, D_FF), D_MODEL ** -0.5),
        "ffn_w2": nrm(ks[24], (L, D_FF, D_MODEL), DN_BETA * D_FF ** -0.5),
        "ln2_g": 1.0 + nrm(ks[25], (L, D_MODEL), 0.02),
        "ln2_b": nrm(ks[26], (L, D_MODEL), 0.02),
    }

def first_block(x, w_in, sgu_ln_g, sgu_ln_b, sgu_w, sgu_b, ssm_lambda_re, ssm_lambda_im, ssm_log_dt,
              ssm_b_re, ssm_b_im, ssm_c_re, ssm_c_im, ssm_d, glu_w, glu_b, w_branch_a, w_branch_b,
              w_branch_c, w_out, ln1_g, ln1_b, ffn_w1, ffn_w3, ffn_w2, ln2_g, ln2_b):
    for l in range(DEPTH):
        mix = hybrid_mixer(x, w_in[l], sgu_ln_g[l], sgu_ln_b[l], sgu_w[l], sgu_b[l],
                           ssm_lambda_re[l], ssm_lambda_im[l], ssm_log_dt[l], ssm_b_re[l], ssm_b_im[l],
                           ssm_c_re[l], ssm_c_im[l], ssm_d[l], glu_w[l], glu_b[l],
                           w_branch_a[l], w_branch_b[l], w_branch_c[l], w_out[l])
        x = layer_norm(DN_ALPHA * x + mix, ln1_g[l], ln1_b[l])
        x = layer_norm(DN_ALPHA * x + swiglu(x, ffn_w1[l], ffn_w3[l], ffn_w2[l]), ln2_g[l], ln2_b[l])
    return x


DEPTH_2 = 1

CTX_LEN = 256
GRID_W = 64
H_M = 8
D_HM = 64
W_M = H_M * D_HM
H_R = 8
D_HR = 64
W_R = H_R * D_HR
MIX_W = W_M + W_R
W_LORA = 64
A_LORA = 64
G_LORA = 128
CONV_K = 3
CONV_CH = 2 * W_M + 3 * W_R
SECTION_WIDTHS = (W_M, W_M, W_R, W_R, W_R, W_M, W_M, 4 * H_M, W_LORA, W_LORA, A_LORA, G_LORA)
IN_COLS_2 = sum(SECTION_WIDTHS)
SPLIT_POINTS = tuple(int(v) for v in np.cumsum(SECTION_WIDTHS)[:-1])
CHUNK = 64
N_GROUPS = 4
E_PER_GROUP = 8
N_EXPERTS = N_GROUPS * E_PER_GROUP
TOP_K_IN_GROUP = 2
D_EXPERT = 512
MOE_BLOCK = 256
ALPHA = (2.0 * DEPTH_2) ** 0.25
BETA = (8.0 * DEPTH_2) ** -0.25
DECAY_SCALE = math.exp(-0.5)
LN_EPS_2 = 1e-6
GN_EPS = 64e-5


def _layernorm(z, gain=None, bias=None):
    zf = z.astype(jnp.float32)
    mu = jnp.mean(zf, -1, keepdims=True)
    var = jnp.mean(jnp.square(zf - mu), -1, keepdims=True)
    y = (zf - mu) * lax.rsqrt(var + LN_EPS_2)
    if gain is not None:
        y = y * gain + bias
    return y.astype(z.dtype)

def _headnorm(z, eps):
    zf = z.astype(jnp.float32)
    mu = jnp.mean(zf, -1, keepdims=True)
    var = jnp.mean(jnp.square(zf - mu), -1, keepdims=True)
    return (zf - mu) * lax.rsqrt(var + eps)

def _modulate(z, shift, scale):
    return _layernorm(z) * (1 + scale) + shift

def _rev_segments(u):
    return jnp.concatenate([jnp.flip(u[:, :CTX_LEN], 1), jnp.flip(u[:, CTX_LEN:], 1)], axis=1)

def _dir_stack(u_fwd, u_bwd):
    return jnp.concatenate([u_fwd, _rev_segments(u_bwd)], axis=0)

def _dir_merge(y):
    b = y.shape[0] // 2
    return y[:b] + _rev_segments(y[b:])

def _conv_grid(u, w, rows):
    b, l, ch = u.shape
    img = u.reshape(b, rows, l // rows, ch)
    out = lax.conv_general_dilated(img, w[:, :, None, :].astype(u.dtype), (1, 1), 'SAME',
                                   dimension_numbers=('NHWC', 'HWIO', 'NHWC'), feature_group_count=ch)
    return out.reshape(b, l, ch)

def _conv_seq(u, w_row):
    ch = u.shape[-1]
    return lax.conv_general_dilated(u, w_row[:, None, :].astype(u.dtype), (1,), 'SAME',
                                    dimension_numbers=('NWC', 'WIO', 'NWC'), feature_group_count=ch)

def _mlstm_chunkwise(q, k, v, log_i, log_f):
    z, t, h, dh = q.shape
    nc = t // CHUNK
    def chunks(a):
        a = a.astype(jnp.float32).reshape((z, nc, CHUNK, h) + a.shape[3:])
        return jnp.swapaxes(jnp.swapaxes(a, 0, 1), 2, 3)
    qc, kc, vc, lic, lfc = chunks(q), chunks(k), chunks(v), chunks(log_i), chunks(log_f)
    tri = jnp.tril(jnp.ones((CHUNK, CHUNK), bool))

    def step(carry, inp):
        c_mat, n_vec, m = carry
        qb, kb, vb, li, lf = inp
        b = jnp.cumsum(lf, -1)
        dmat = jnp.where(tri, b[..., :, None] - b[..., None, :] + li[..., None, :], -jnp.inf)
        m_inter = b + m[..., None]
        m_t = jnp.maximum(m_inter, jnp.max(dmat, -1))
        s = jnp.einsum('zhtd,zhsd->zhts', qb, kb) * jnp.exp(dmat - m_t[..., None])
        inter = jnp.exp(m_inter - m_t)
        num = inter[..., None] * jnp.einsum('zhtd,zhde->zhte', qb, c_mat) + jnp.einsum('zhts,zhse->zhte', s, vb)
        den = inter * jnp.einsum('zhtd,zhd->zht', qb, n_vec) + jnp.sum(s, -1)
        h_out = num / jnp.maximum(jnp.abs(den), jnp.exp(-m_t))[..., None]
        b_last = b[..., -1]
        g = b_last[..., None] - b + li
        m_new = jnp.maximum(b_last + m, jnp.max(g, -1))
        wts = jnp.exp(g - m_new[..., None])
        decay = jnp.exp(b_last + m - m_new)
        c_mat = decay[..., None, None] * c_mat + jnp.einsum('zhs,zhsd,zhse->zhde', wts, kb, vb)
        n_vec = decay[..., None] * n_vec + jnp.einsum('zhs,zhsd->zhd', wts, kb)
        return (c_mat, n_vec, m_new), h_out

    init = (jnp.zeros((z, h, dh, dh), jnp.float32), jnp.zeros((z, h, dh), jnp.float32), jnp.zeros((z, h), jnp.float32))
    _, hs = lax.scan(step, init, (qc, kc, vc, lic, lfc))
    return jnp.swapaxes(jnp.swapaxes(hs, 2, 3), 0, 1).reshape(z, t, h, dh)

def _mlstm_group(mq, mk, mv, mo, gates, b_i, b_f, norm_w):
    b, t, _ = mq.shape
    q = jax.nn.silu(mq).reshape(b, t, H_M, D_HM)
    k = jax.nn.silu(mk).reshape(b, t, H_M, D_HM) * (D_HM ** -0.5)
    v = mv.reshape(b, t, H_M, D_HM)
    gt = gates.astype(jnp.float32).reshape(b, t, 4, H_M)
    li_f = gt[:, :, 0] + b_i[0]
    lf_f = jax.nn.log_sigmoid(gt[:, :, 1] + b_f[0])
    li_b = gt[:, :, 2] + b_i[1]
    lf_b = jax.nn.log_sigmoid(gt[:, :, 3] + b_f[1])
    h = _mlstm_chunkwise(_dir_stack(q, q), _dir_stack(k, k), _dir_stack(v, v),
                         _dir_stack(li_f, li_b), _dir_stack(lf_f, lf_b))
    h = _headnorm(_dir_merge(h), LN_EPS_2) * norm_w.reshape(H_M, D_HM)
    return jax.nn.sigmoid(mo) * h.reshape(b, t, W_M)

def _rwkv7_scan(r, w, k, v, kh, a):
    z, t, h, n = r.shape
    seq = tuple(jnp.moveaxis(s.astype(jnp.float32), 1, 0) for s in (r, w, k, v, kh, a))

    def step(state, inp):
        r_t, w_t, k_t, v_t, kh_t, a_t = inp
        removed = jnp.einsum('zhvk,zhk->zhv', state, kh_t)
        state = (state * w_t[:, :, None, :] - removed[..., None] * (kh_t * a_t)[:, :, None, :]
                 + v_t[..., None] * k_t[:, :, None, :])
        return state, jnp.einsum('zhvk,zhk->zhv', state, r_t)

    _, y = lax.scan(step, jnp.zeros((z, h, n, n), jnp.float32), seq)
    return jnp.moveaxis(y, 0, 1)

def _rwkv7_group(rr, rk, rv, lw_f, lw_b, la, lg, w0, w_b_mat, a0, a_b_mat, g_b_mat, kk, ka, bonus_w, gn_w, gn_b):
    b, t, _ = rr.shape
    shp = (b, t, H_R, D_HR)
    w_fwd = jnp.exp(-DECAY_SCALE * jax.nn.sigmoid((w0[0] + jnp.tanh(lw_f) @ w_b_mat[0]).astype(jnp.float32)))
    w_bwd = jnp.exp(-DECAY_SCALE * jax.nn.sigmoid((w0[1] + jnp.tanh(lw_b) @ w_b_mat[1]).astype(jnp.float32)))
    a = jax.nn.sigmoid(a0 + la @ a_b_mat)
    g = jax.nn.sigmoid(lg) @ g_b_mat
    kap = (rk * kk).reshape(shp).astype(jnp.float32)
    kh = kap / jnp.maximum(jnp.sqrt(jnp.sum(jnp.square(kap), -1, keepdims=True)), 1e-12)
    kmod = (rk * (1 + (a - 1) * ka)).reshape(shp)
    r = rr.reshape(shp)
    v = rv.reshape(shp)
    a_h = a.reshape(shp)
    y = _rwkv7_scan(_dir_stack(r, r), _dir_stack(w_fwd.reshape(shp), w_bwd.reshape(shp)), _dir_stack(kmod, kmod),
                    _dir_stack(v, v), _dir_stack(kh, kh), _dir_stack(a_h, a_h))
    y = _headnorm(_dir_merge(y), GN_EPS) * gn_w.reshape(H_R, D_HR) + gn_b.reshape(H_R, D_HR)
    bonus = jnp.sum(r * kmod * bonus_w, -1, keepdims=True) * v
    return (y + bonus).reshape(b, t, W_R) * g

def _mixer(h_ctx, h_lat, rows, w_in, conv_w, m_bias_i, m_bias_f, m_norm_w, r_w0, r_wB, r_a0, r_aB, r_gB,
           r_kk, r_ka, r_bonus, r_norm_w, r_norm_b):
    p_ctx = h_ctx @ w_in
    p_lat = h_lat @ w_in
    p_ctx = jnp.concatenate([_conv_seq(p_ctx[..., :CONV_CH], conv_w[CONV_K // 2]), p_ctx[..., CONV_CH:]], -1)
    p_lat = jnp.concatenate([_conv_grid(p_lat[..., :CONV_CH], conv_w, rows), p_lat[..., CONV_CH:]], -1)
    u = jnp.concatenate([p_ctx, p_lat], axis=1)
    mq, mk, rr, rk, rv, mv, mo, gates, lw_f, lw_b, la, lg = jnp.split(u, SPLIT_POINTS, axis=-1)
    out_m = _mlstm_group(mq, mk, mv, mo, gates, m_bias_i, m_bias_f, m_norm_w)
    out_r = _rwkv7_group(rr, rk, rv, lw_f, lw_b, la, lg, r_w0, r_wB, r_a0, r_aB, r_gB, r_kk, r_ka, r_bonus,
                         r_norm_w, r_norm_b)
    return jnp.concatenate([out_m.astype(out_r.dtype), out_r], -1)

def _hier_moe(h, rt_g, rt_g_b, rt_e, rt_e_b, ex_gate, ex_up, ex_down):
    b, t, d = h.shape
    tok = h.reshape(b * t, d)
    n = tok.shape[0]
    lg = (tok @ rt_g + rt_g_b).astype(jnp.float32)
    p_grp = jax.nn.softmax(lg, axis=-1)
    grp = jnp.argmax(lg, axis=-1).astype(jnp.int32)
    p_top = jnp.take_along_axis(p_grp, grp[:, None], axis=-1)
    le = (tok @ rt_e + rt_e_b).astype(jnp.float32).reshape(n, N_GROUPS, E_PER_GROUP)
    le_grp = jnp.take_along_axis(le, jnp.broadcast_to(grp[:, None, None], (n, 1, E_PER_GROUP)), axis=1)[:, 0]
    top_val, top_idx = lax.top_k(le_grp, TOP_K_IN_GROUP)
    wts = jax.nn.softmax(top_val, axis=-1) * p_top
    e_flat = (grp[:, None] * E_PER_GROUP + top_idx.astype(jnp.int32)).reshape(-1)
    w_flat = wts.reshape(-1)
    t_flat = jnp.repeat(jnp.arange(n, dtype=jnp.int32), TOP_K_IN_GROUP)
    order = jnp.argsort(e_flat)
    e_s, t_s, w_s = e_flat[order], t_flat[order], w_flat[order]
    counts = jnp.zeros((N_EXPERTS,), jnp.int32).at[e_flat].add(1)
    starts = jnp.cumsum(counts) - counts
    padded = (counts + MOE_BLOCK - 1) // MOE_BLOCK * MOE_BLOCK
    pad_ends = jnp.cumsum(padded)
    pad_starts = pad_ends - padded
    dest = pad_starts[e_s] + jnp.arange(e_s.shape[0], dtype=jnp.int32) - starts[e_s]
    n_pairs = n * TOP_K_IN_GROUP
    buf = (-(-n_pairs // MOE_BLOCK) + N_EXPERTS) * MOE_BLOCK
    tok_buf = jnp.full((buf,), n, jnp.int32).at[dest].set(t_s)
    w_buf = jnp.zeros((buf,), w_s.dtype).at[dest].set(w_s)
    n_blk = buf // MOE_BLOCK
    blk_exp = jnp.minimum(jnp.searchsorted(pad_ends, jnp.arange(n_blk, dtype=jnp.int32) * MOE_BLOCK, side='right'),
                          N_EXPERTS - 1)
    tok_pad = jnp.concatenate([tok, jnp.zeros((1, d), tok.dtype)], 0)

    def expert_block(args):
        idx, w, e = args
        xb = tok_pad[idx]
        hb = jax.nn.silu(xb @ ex_gate[e]) * (xb @ ex_up[e])
        return (hb @ ex_down[e]) * w[:, None]

    y = lax.map(expert_block, (tok_buf.reshape(n_blk, MOE_BLOCK), w_buf.reshape(n_blk, MOE_BLOCK), blk_exp))
    out = jnp.zeros((n + 1, d), y.dtype).at[tok_buf].add(y.reshape(buf, d))
    return out[:n].reshape(b, t, d).astype(h.dtype)

def second_inputs(seed: int = 0) -> dict:
    key = jax.random.key(seed)
    ks = jax.random.split(key, 40)
    def nrm(k, shape, s):
        return jax.random.normal(k, shape, jnp.float32) * s
    L = DEPTH_2
    return {
        'x': nrm(ks[0], (BATCH, SEQ, D_MODEL), 1.0),
        'c': nrm(ks[1], (BATCH, D_MODEL), 1.0),
        'ctx': nrm(ks[2], (BATCH, CTX_LEN, D_MODEL), 1.0),
        'c_ctx': nrm(ks[3], (D_MODEL,), 1.0),
        'w_ada': nrm(ks[4], (L, D_MODEL, 6 * D_MODEL), D_MODEL ** -0.5),
        'b_ada': nrm(ks[5], (L, 6 * D_MODEL), 0.02),
        'w_in': nrm(ks[6], (L, D_MODEL, IN_COLS_2), D_MODEL ** -0.5),
        'conv_w': nrm(ks[7], (L, CONV_K, CONV_K, CONV_CH), 0.3),
        'm_bias_i': nrm(ks[8], (L, 2, H_M), 0.5),
        'm_bias_f': 3.0 + nrm(ks[9], (L, 2, H_M), 0.5),
        'm_norm_w': 1.0 + nrm(ks[10], (L, W_M), 0.05),
        'r_w0': nrm(ks[11], (L, 2, W_R), 0.5),
        'r_wB': nrm(ks[12], (L, 2, W_LORA, W_R), W_LORA ** -0.5),
        'r_a0': nrm(ks[13], (L, W_R), 0.5),
        'r_aB': nrm(ks[14], (L, A_LORA, W_R), A_LORA ** -0.5),
        'r_gB': nrm(ks[15], (L, G_LORA, W_R), G_LORA ** -0.5),
        'r_kk': 0.85 + nrm(ks[16], (L, W_R), 0.05),
        'r_ka': 1.0 + nrm(ks[17], (L, W_R), 0.05),
        'r_bonus': nrm(ks[18], (L, H_R, D_HR), 0.1),
        'r_norm_w': 1.0 + nrm(ks[19], (L, W_R), 0.05),
        'r_norm_b': nrm(ks[20], (L, W_R), 0.02),
        'w_out': nrm(ks[21], (L, MIX_W, D_MODEL), BETA * MIX_W ** -0.5),
        'ln1_g': 1.0 + nrm(ks[22], (L, D_MODEL), 0.05),
        'ln1_b': nrm(ks[23], (L, D_MODEL), 0.02),
        'ln2_g': 1.0 + nrm(ks[24], (L, D_MODEL), 0.05),
        'ln2_b': nrm(ks[25], (L, D_MODEL), 0.02),
        'rt_g': nrm(ks[26], (L, D_MODEL, N_GROUPS), D_MODEL ** -0.5),
        'rt_g_b': nrm(ks[27], (L, N_GROUPS), 0.01),
        'rt_e': nrm(ks[28], (L, D_MODEL, N_EXPERTS), D_MODEL ** -0.5),
        'rt_e_b': nrm(ks[29], (L, N_EXPERTS), 0.01),
        'ex_gate': nrm(ks[30], (L, N_EXPERTS, D_MODEL, D_EXPERT), D_MODEL ** -0.5),
        'ex_up': nrm(ks[31], (L, N_EXPERTS, D_MODEL, D_EXPERT), D_MODEL ** -0.5),
        'ex_down': nrm(ks[32], (L, N_EXPERTS, D_EXPERT, D_MODEL), BETA * D_EXPERT ** -0.5),
    }

def second_block(x, c, ctx, c_ctx, w_ada, b_ada, w_in, conv_w, m_bias_i, m_bias_f, m_norm_w, r_w0, r_wB, r_a0, r_aB,
              r_gB, r_kk, r_ka, r_bonus, r_norm_w, r_norm_b, w_out, ln1_g, ln1_b, ln2_g, ln2_b, rt_g, rt_g_b, rt_e,
              rt_e_b, ex_gate, ex_up, ex_down):
    rows = x.shape[1] // GRID_W
    for l in range(DEPTH_2):
        mod = jax.nn.silu(c) @ w_ada[l] + b_ada[l]
        mod_c = jax.nn.silu(c_ctx) @ w_ada[l] + b_ada[l]
        sh1, sc1, g1, sh2, sc2, g2 = jnp.split(mod[:, None, :], 6, axis=-1)
        sh1c, sc1c, g1c, sh2c, sc2c, g2c = jnp.split(mod_c, 6)
        mixed = _mixer(_modulate(ctx, sh1c, sc1c), _modulate(x, sh1, sc1), rows, w_in[l], conv_w[l], m_bias_i[l],
                       m_bias_f[l], m_norm_w[l], r_w0[l], r_wB[l], r_a0[l], r_aB[l], r_gB[l], r_kk[l], r_ka[l],
                       r_bonus[l], r_norm_w[l], r_norm_b[l])
        x = _layernorm(ALPHA * x + g1 * (mixed[:, CTX_LEN:] @ w_out[l]), ln1_g[l], ln1_b[l])
        ffn = _hier_moe(_modulate(x, sh2, sc2), rt_g[l], rt_g_b[l], rt_e[l], rt_e_b[l], ex_gate[l], ex_up[l], ex_down[l])
        x = _layernorm(ALPHA * x + g2 * ffn, ln2_g[l], ln2_b[l])
        if l + 1 < DEPTH_2:
            ctx = _layernorm(ALPHA * ctx + g1c * (mixed[:, :CTX_LEN] @ w_out[l]), ln1_g[l], ln1_b[l])
            ffn_c = _hier_moe(_modulate(ctx, sh2c, sc2c), rt_g[l], rt_g_b[l], rt_e[l], rt_e_b[l], ex_gate[l],
                              ex_up[l], ex_down[l])
            ctx = _layernorm(ALPHA * ctx + g2c * ffn_c, ln2_g[l], ln2_b[l])
    return x


def setup_inputs(seed=0):
    out = dict(first_inputs(seed))
    for name, value in second_inputs(seed + 1).items():
        if name != "x":
            out[name + "_2"] = value
    return out


def reference(
    x, w_in, sgu_ln_g, sgu_ln_b, sgu_w, sgu_b, ssm_lambda_re, ssm_lambda_im, ssm_log_dt,
    ssm_b_re, ssm_b_im, ssm_c_re, ssm_c_im, ssm_d, glu_w, glu_b, w_branch_a, w_branch_b,
    w_branch_c, w_out, ln1_g, ln1_b, ffn_w1, ffn_w3, ffn_w2, ln2_g, ln2_b, c_2, ctx_2, c_ctx_2,
    w_ada_2, b_ada_2, w_in_2, conv_w_2, m_bias_i_2, m_bias_f_2, m_norm_w_2, r_w0_2, r_wB_2,
    r_a0_2, r_aB_2, r_gB_2, r_kk_2, r_ka_2, r_bonus_2, r_norm_w_2, r_norm_b_2, w_out_2, ln1_g_2,
    ln1_b_2, ln2_g_2, ln2_b_2, rt_g_2, rt_g_b_2, rt_e_2, rt_e_b_2, ex_gate_2, ex_up_2,
    ex_down_2,
):
    x = first_block(
        x, w_in, sgu_ln_g, sgu_ln_b, sgu_w, sgu_b, ssm_lambda_re, ssm_lambda_im, ssm_log_dt,
        ssm_b_re, ssm_b_im, ssm_c_re, ssm_c_im, ssm_d, glu_w, glu_b, w_branch_a, w_branch_b,
        w_branch_c, w_out, ln1_g, ln1_b, ffn_w1, ffn_w3, ffn_w2, ln2_g, ln2_b,
    )
    return second_block(
        x, c_2, ctx_2, c_ctx_2, w_ada_2, b_ada_2, w_in_2, conv_w_2, m_bias_i_2, m_bias_f_2,
        m_norm_w_2, r_w0_2, r_wB_2, r_a0_2, r_aB_2, r_gB_2, r_kk_2, r_ka_2, r_bonus_2,
        r_norm_w_2, r_norm_b_2, w_out_2, ln1_g_2, ln1_b_2, ln2_g_2, ln2_b_2, rt_g_2, rt_g_b_2,
        rt_e_2, rt_e_b_2, ex_gate_2, ex_up_2, ex_down_2,
    )


_drawn_inputs = setup_inputs


def setup_inputs(seed=0):
    import zlib

    import numpy as np

    out = dict(_drawn_inputs(seed))
    spreads = {}
    factors = {'sgu_ln_g': 5.478,
     'sgu_ln_b': 7.02,
     'sgu_b': 4.491,
     'ssm_lambda_re': 64.0,
     'ssm_lambda_im': 28.896,
     'ssm_log_dt': 27.24,
     'ssm_b_re': 37.44,
     'ssm_b_im': 35.856,
     'ssm_c_re': 23.56,
     'ssm_c_im': 30.296,
     'glu_b': 25.149,
     'm_bias_i_2': 3.523,
     'm_norm_w_2': 3.095,
     'r_kk_2': 35.754,
     'r_ka_2': 3.331,
     'r_norm_w_2': 3.056,
     'r_norm_b_2': 14.485,
     'ln2_b_2': 2.823,
     'rt_g_b_2': 4.578,
     'rt_e_b_2': 12.711}
    for name, (base, spread) in spreads.items():
        noise = np.random.default_rng([zlib.crc32(name.encode()), seed]).standard_normal(out[name].shape)
        drawn = base * np.exp(spread * noise) if base else spread * noise
        out[name] = jnp.asarray(drawn.astype(out[name].dtype))
    for name, factor in factors.items():
        out[name] = (out[name] * factor).astype(out[name].dtype)
    return out
```

```python
import math
from contextlib import ExitStack

import numpy as np

import concourse.bass as bass
from concourse import mybir

ALU = mybir.AluOpType
ACT = mybir.ActivationFunctionType
AX_X = mybir.AxisListType.X
F32 = mybir.dt.float32

P = 128
D = 1024
DC = D // P
T = 256
TT = T // P
DEPTH = 2
BANK = 512
BANKS = 8

W5 = 512
WC = W5 // P
ST = 16
HEADS = 8
HD = 64
D_FF = 2816
FC = D_FF // P
IN_COLS = 2 * W5 + W5 + 3 * W5 + 3 * D
DN_ALPHA = (2 * DEPTH) ** 0.25
LN_EPS = 1e-5
TWO_PI = 6.283185
MAGIC = 1.5 * 2.0 ** 23
MASKED = -1e30

SLOTS = 3
SLOT = 4096
W_IN_ORDER = [2, 1, 0, 3, 4, 5] + list(range(6, 12))
FFN_COLS = 256
FFN_UNITS = D_FF // FFN_COLS
W2_ROWS = 4
DMAS = {"w13": 2}
W2_UNITS = -(-FC // W2_ROWS)


def layer_units():
    units = [("w_in", c) for c in W_IN_ORDER]
    units += [("glu_w", 0), ("w_a", 0), ("w_c", 0), ("w_b", 0), ("w_out", 0), ("w_out", 1)]
    units += [("w13", c) for c in range(FFN_UNITS)]
    units += [("w2", c) for c in range(W2_UNITS)]
    return units + [None] * (-len(units) % SLOTS)


def layer_groups():
    keys = [("xT", q) for q in range(4)] + [("vec", 0), ("wT", 0), ("CT", 0), ("CT", 1)]
    keys += [("ssm", i) for i in range(2)] + [("v", i) for i in range(2)] + [("u", i) for i in range(2)]
    keys += [("BT", 0), ("BT", 1)]
    keys += [("q", i) for i in range(2)]
    keys += [("bu", 0, c) for c in range(2)]
    keys += [("k", i) for i in range(2)] + [("av", i) for i in range(2)]
    keys += [("mix", i) for i in range(2)]
    for n in range(HEADS):
        keys += [("sc", n)]
        if n < 7:
            keys += [("bu", n + 1, c) for c in range(2)]
        keys += [("gate", g) for g in GATES_WITH[n]]
        if n % 2 == 1:
            keys += [("y", n // 2)]
        keys += [("pT", n)]
        keys += [("o", n // 2)] if n % 2 == 1 else []
    keys += [("glu", i) for i in range(2)]
    for x in (0, 2, 1):
        keys += [("br", x, i) for i in range(4)]
    keys += [("mo", tt, hf) for hf in range(2) for tt in range(TT)]
    keys += [("x1T", q) for q in range(4)]
    for c in range(FFN_UNITS):
        keys += [("f1", c), ("f3", c)]
    keys += [("f2", tt, hf) for tt in range(TT) for hf in range(2)]
    return keys


def layer_closes():
    closes = {("ssm", 1): ("w_in", 2), ("v", 1): ("w_in", 1), ("u", 1): ("w_in", 0), ("q", 1): ("w_in", 3),
              ("k", 1): ("w_in", 4), ("av", 1): ("w_in", 5), ("glu", 1): ("glu_w", 0), ("br", 0, 3): ("w_a", 0),
              ("br", 1, 3): ("w_b", 0), ("br", 2, 3): ("w_c", 0)}
    closes |= {("gate", 2 * c + 1): ("w_in", 6 + c) for c in range(6)}
    closes |= {("mo", TT - 1, hf): ("w_out", hf) for hf in range(2)}
    closes |= {("f3", c): ("w13", c) for c in range(FFN_UNITS)}
    return closes | {("f2", TT - 1, 1): ("w2", W2_UNITS - 1)}


GATES_WITH = [[0], [1, 2], [3], [4, 5], [6], [7, 8], [9], [10, 11]]


class Phase:

    def __init__(self, name, times, groups, units, closes):
        self.name, self.times, self.groups, self.units, self.closes = name, times, groups, units, closes


class Tickets:

    def __init__(self, phases, pick, n, counted=lambda ph, key: 1):
        self.at, base = {}, [0] * n
        for ph in phases:
            per = [0] * n
            keys = pick(ph)
            assert n == BANKS or ph.times == 1 or len(keys) % n == 0
            here = {}
            for i, key in enumerate(keys):
                if key is None:
                    continue
                per[i % n] += counted(ph, key)
                assert key not in self.at and key not in here, key
                here[key] = (i % n, base[i % n] + per[i % n])
            self.at |= {key: (b, first, per[b]) for key, (b, first) in here.items()}
            base = [x + ph.times * y for x, y in zip(base, per)]

    def value(self, key, it, ago=0):
        b, first, per = self.at[key]
        assert ago == 0 or first > ago * per, key
        return b, it * per + (first - ago * per)


class Chain:

    def __init__(self, sem, base=0, it=0, per=0):
        self.sem, self.base, self.it, self.per, self.n = sem, base, it, per, 0

    def count(self):
        self.n += 1
        return self.it * self.per + (self.base + self.n)

    def end(self, times=1):
        assert times == 1 or self.per == self.n, f"a run of the body has {self.n} steps"
        return self.base + times * self.n


class Kit:

    def __init__(self, nc, ctx, phases, events):
        self.closes = {g: u for ph in phases for g, u in ph.closes.items()}
        self.banks = Tickets(phases, lambda ph: ph.groups, BANKS)
        self.fills = Tickets(phases, lambda ph: ph.groups, BANKS, lambda ph, key: key not in ph.closes)
        self.ring = Tickets(phases, lambda ph: ph.units, SLOTS)
        self.landings = Tickets(phases, lambda ph: ph.units, SLOTS, lambda ph, key: DMAS.get(key[0], 1))
        sem = lambda name: ctx.enter_context(nc.semaphore(name))
        self.bank_filled = [sem(f"bank{b}_filled") for b in range(BANKS)]
        self.bank_drained = [sem(f"bank{b}_drained") for b in range(BANKS)]
        self.slot_landed = [sem(f"slot{s}_landed") for s in range(SLOTS)]
        self.slot_used = [sem(f"slot{s}_used") for s in range(SLOTS)]
        self.sync_steps = sem("sync_steps")
        self.per = dict(events)
        self.sem = {name: sem(name) for name in events}
        self.psum = ctx.enter_context(nc.psum_tensor("psum", [P, BANKS, BANK], F32))
        self.slot = ctx.enter_context(nc.sbuf_tensor("ring", [P, SLOTS, SLOT], F32))

    def bank(self, key):
        return self.psum[:, self.banks.at[key][0], :]

    def full(self, key):
        return self.used_up(self.closes[key]) if key in self.closes else self.bank_filled[self.banks.at[key][0]]

    def full_count(self, key, it=0, ago=0):
        if key in self.closes:
            return self.ring.value(self.closes[key], it, ago)[1] + 1
        return self.fills.value(key, it, ago)[1]

    def empty(self, key):
        return self.bank_drained[self.banks.at[key][0]]

    def empty_count(self, key, it=0):
        return self.banks.value(key, it)[1]

    def drained_count(self, key, it=0, ago=0):
        return self.banks.value(key, it, ago)[1] + 1

    def used_up(self, key):
        return self.slot_used[self.ring.at[key][0]]

    def free_count(self, key, it=0):
        return self.ring.value(key, it)[1]

    def landed(self, key):
        return self.slot_landed[self.ring.at[key][0]]

    def landed_count(self, key, it=0):
        _, first, per = self.landings.at[key]
        return it * (per * 16) + first * 16

    def weights(self, key, k, n):
        return self.slot[:, self.ring.at[key][0], 0:k * n].rearrange("p (k n) -> p k n", k=k)

    def slot_like(self, key, src):
        return self.weights(key, src.shape[1], src.shape[2])

    def count(self, name, it=0, n=None):
        unit = 16 if name.startswith("dma_") else 1
        n = self.per[name] if n is None else n
        return it * (self.per[name] * unit) + n * unit


LAYER_EVENTS = dict(
    params_free=1, dma_params=29, dma_ln=4, x_in=1, dt_row=1, ssm_dt=1, ssm_angle=1, ssm_trig=1, ssm_bbar=1,
    angle=8, cos_sin=8, scanned=8, h_ready=8, y_gelu=4, glu_out=1,
    v_var=1, v_std=1, v_norm=1, v_ready=1, tril=1,
    neg_max=8, exped=8, probs=8, merged=4, x1_var=2, x1_std=2, x1=2, x2_var=2, x2_std=2,
)


def layer_sync(sp, K, A):
    with sp.Fori(0, DEPTH) as l:
        one = bass.ds(l, 1)

        def par(dst, src, name="dma_params"):
            sp.dma_start(dst, src).then_inc(K.sem[name], 16)

        sp.wait_ge(K.sem["params_free"], K.count("params_free", l))
        sp.sem_inc(K.sync_steps, 1)
        par(K.vrows[0:ST, :], A["ssm_lambda_re"][one].rearrange("a (t g) p -> (a t) (g p)", g=2))
        par(K.vrows[32:32 + ST, :], A["ssm_lambda_im"][one].rearrange("a (t g) p -> (a t) (g p)", g=2))
        par(K.dtrow[64:64 + ST, :], A["ssm_log_dt"][one].rearrange("a (t g) -> (a t) g", g=2))
        par(K.vrows[96:96 + WC, :], A["ssm_d"][one].rearrange("a (t g) -> (a t) g", g=P))
        par(K.vrows[96 + WC:96 + 2 * WC, :], A["glu_b"][one].rearrange("a (t g) -> (a t) g", g=P))
        for nat, src in ((K.b_nat_re, A["ssm_b_re"]), (K.b_nat_im, A["ssm_b_im"])):
            for g in range(2):
                par(nat[g * 64:g * 64 + 64, :, g * 16:g * 16 + 16],
                    src[one].rearrange("a (t g) p h -> g p (a t) h", g=2)[g])
        for nat, src in ((K.c_nat_re, A["ssm_c_re"]), (K.c_nat_im, A["ssm_c_im"])):
            for g in range(2):
                for j in range(4):
                    q = j * 32 + g * 16
                    par(nat[q:q + 16, :, g * 64:g * 64 + 64],
                        src[one].rearrange("a (b j g) h p -> j g h (a b) p", j=4, g=2)[j, g])
        par(K.w_nat, A["sgu_w"][one].rearrange("a g t s -> t (a g) s"))
        par(K.sgu_bias[0:1, :], A["sgu_b"][one].rearrange("a g t -> a (g t)"))
        par(K.v_gain, A["sgu_ln_g"][one, :].broadcast_to([P, W5]))
        par(K.v_bias, A["sgu_ln_b"][one, :].broadcast_to([P, W5]))
        rows = lambda a: a[one].rearrange("a (k p) n -> p (a k) n", p=P)
        src = {"glu_w": A["glu_w"], "w_a": A["w_branch_a"], "w_b": A["w_branch_b"], "w_c": A["w_branch_c"]}
        for kind, c in filter(None, layer_units()):
            if kind == "w_in":
                sp.wait_ge(K.used_up((kind, c)), K.free_count((kind, c), l))
                sp.sem_inc(K.sync_steps, 1)
                weights = rows(A["w_in"])[:, :, c * BANK:(c + 1) * BANK]
                sp.dma_start(K.slot_like((kind, c), weights), weights).then_inc(K.landed((kind, c)), 16)
            elif kind in src:
                sp.wait_ge(K.used_up((kind, c)), K.free_count((kind, c), l))
                sp.sem_inc(K.sync_steps, 1)
                weights = rows(src[kind])
                sp.dma_start(K.slot_like((kind, c), weights), weights).then_inc(K.landed((kind, c)), 16)
            elif kind == "w_out":
                if c == 0:
                    sp.wait_ge(K.empty(("y", 3)), K.drained_count(("y", 3), l))
                    sp.sem_inc(K.sync_steps, 1)
                    for i, vec in enumerate((A["ln1_g"], A["ln1_b"], A["ln2_g"], A["ln2_b"])):
                        sp.dma_start(K.ln_rows[:, i, :], vec[one, :].broadcast_to([P, D])).then_inc(K.sem["dma_ln"], 16)
                sp.wait_ge(K.used_up((kind, c)), K.free_count((kind, c), l))
                sp.sem_inc(K.sync_steps, 1)
                weights = rows(A["w_out"])[:, :, c * BANK:(c + 1) * BANK]
                sp.dma_start(K.slot_like((kind, c), weights), weights).then_inc(K.landed((kind, c)), 16)
            elif kind == "w13":
                sp.wait_ge(K.used_up((kind, c)), K.free_count((kind, c), l))
                sp.sem_inc(K.sync_steps, 1)
                both = K.weights((kind, c), 2 * DC, FFN_COLS).rearrange("p (w k) n -> p w k n", w=2)
                for w, m in enumerate((A["ffn_w1"], A["ffn_w3"])):
                    sp.dma_start(both[:, w], rows(m)[:, :, c * FFN_COLS:(c + 1) * FFN_COLS]).then_inc(K.landed((kind, c)), 16)
            else:
                sp.wait_ge(K.used_up((kind, c)), K.free_count((kind, c), l))
                sp.sem_inc(K.sync_steps, 1)
                weights = rows(A["ffn_w2"])[:, c * W2_ROWS:min((c + 1) * W2_ROWS, FC), :]
                sp.dma_start(K.slot_like((kind, c), weights), weights).then_inc(K.landed((kind, c)), 16)


def layer_tensor(pe, K):
    ident = K.ident

    def cols(n, k=2):
        return lambda bank: bank[:, 0:n * k].rearrange("p (k n) -> p k n", k=k)

    pairs = cols(T)

    with pe.Fori(0, DEPTH) as l:

        def turn(name, key, src):
            for q in range(4):
                pe.wait_ge(K.empty((key, q)), K.empty_count((key, q), l))
                bank = pairs(K.bank((key, q)))
                for j in range(2):
                    for tt in range(TT):
                        if name:
                            pe.wait_ge(K.sem[name], K.count(name, l, tt + 1))
                        ins = pe.transpose(bank[:, j, tt * P:(tt + 1) * P],
                                           src[:, tt, (2 * q + j) * P:(2 * q + j + 1) * P], ident)
                ins.then_inc(K.full((key, q)), 1)

        def channels(name, i, w, moving, k=DC, j0=None):
            key = name + (i,)
            pe.wait_ge(K.empty(key), K.empty_count(key, l))
            bank = pairs(K.bank(key))
            for j in range(2):
                c = (2 * i if j0 is None else j0) + j
                for kc in range(k):
                    ins = pe.matmul(bank[:, j, :], w[:, kc, c * P:(c + 1) * P], moving[:, kc, :],
                                    start=kc == 0, stop=kc == k - 1)
            ins.then_inc(K.full(key), 1)

        def tokens(name, unit):
            pe.wait_ge(K.landed(("w_in", unit)), K.landed_count(("w_in", unit), l))
            w = K.weights(("w_in", unit), DC, BANK)
            for tt in range(TT):
                pe.wait_ge(K.empty((name, tt)), K.empty_count((name, tt), l))
                bank = K.bank((name, tt))
                for kc in range(DC):
                    ins = pe.matmul(bank, K.xT[:, kc, tt * P:(tt + 1) * P], w[:, kc, :], start=kc == 0, stop=kc == DC - 1)
                ins.then_inc(K.full((name, tt)), 1)

        def project(name, unit):
            pe.wait_ge(K.landed(("w_in", unit)), K.landed_count(("w_in", unit), l))
            w = K.weights(("w_in", unit), DC, BANK)
            for i in range(2):
                channels((name,), i, w, K.xT)

        pe.wait_ge(K.sem["x_in"], K.count("x_in", l))
        turn(None, "xT", K.x_tok)
        pe.wait_ge(K.sem["dma_params"], K.count("dma_params", l))
        pe.wait_ge(K.empty(("vec", 0)), K.empty_count(("vec", 0), l))
        bank = K.bank(("vec", 0))
        pe.wait_ge(K.sem["dt_row"], K.count("dt_row", l))
        pe.transpose(bank[:, 0:P], K.vrows, ident).then_inc(K.full(("vec", 0)), 1)
        pe.wait_ge(K.sem["tril"], K.count("tril", l))
        pe.wait_ge(K.empty(("wT", 0)), K.empty_count(("wT", 0), l))
        bank = K.bank(("wT", 0))
        for g in range(WC):
            ins = pe.transpose(bank[:, g * P:(g + 1) * P], K.w_nat[:, g, :], ident)
        ins.then_inc(K.full(("wT", 0)), 1)
        for i, nat in enumerate((K.c_nat_re, K.c_nat_im)):
            pe.wait_ge(K.empty(("CT", i)), K.empty_count(("CT", i), l))
            bank = K.bank(("CT", i))
            for b in range(WC):
                ins = pe.transpose(bank[:, b * P:(b + 1) * P], nat[:, b, :], ident)
            ins.then_inc(K.full(("CT", i)), 1)

        for q in range(4):
            pe.wait_ge(K.empty(("xT", q)), K.drained_count(("xT", q), l))
        project("ssm", 2)
        tokens("v", 1)
        project("u", 0)
        pe.wait_ge(K.sem["ssm_bbar"], K.count("ssm_bbar", l))
        for i, nat in enumerate((K.bbar_re, K.bbar_im)):
            pe.wait_ge(K.empty(("BT", i)), K.empty_count(("BT", i), l))
            bank = K.bank(("BT", i))
            for b in range(WC):
                ins = pe.transpose(bank[:, b * P:(b + 1) * P], nat[:, 4 * b:4 * b + 4, :].rearrange("p t h -> p (t h)"), ident)
            ins.then_inc(K.full(("BT", i)), 1)
        project("q", 3)

        def state_inputs(n):
            b, j0 = n // 2, 2 * (n % 2)
            if n == 0:
                for i in range(2):
                    pe.wait_ge(K.empty(("BT", i)), K.drained_count(("BT", i), l))
                    pe.wait_ge(K.empty(("ssm", i)), K.drained_count(("ssm", i), l))
            for i, w in enumerate((K.bT_re, K.bT_im)):
                pe.wait_ge(K.empty(("bu", n, i)), K.empty_count(("bu", n, i), l))
                bank = pairs(K.bank(("bu", n, i)))
                for j in range(2):
                    ins = pe.matmul(bank[:, j, :], w[:, j0 + j, b * P:(b + 1) * P], K.zssm[:, b, :], start=True, stop=True)
                ins.then_inc(K.full(("bu", n, i)), 1)

        def state_outputs(b):
            if b == 0:
                for i in range(2):
                    pe.wait_ge(K.empty(("CT", i)), K.drained_count(("CT", i), l))
            pe.wait_ge(K.empty(("y", b)), K.empty_count(("y", b), l))
            bank = K.bank(("y", b))
            for half in range(2):
                pe.wait_ge(K.sem["h_ready"], K.count("h_ready", l, 2 * b + half + 1))
                for j in range(2):
                    jj = 2 * half + j
                    for i, (w, h) in enumerate(((K.cT_re, K.h_re), (K.cT_im, K.h_im))):
                        ins = pe.matmul(bank[jj * 32:jj * 32 + 32, 0:T], w[:, b, jj * 32:jj * 32 + 32],
                                        h[:, half, j * T:(j + 1) * T], start=i == 0, stop=i == 1)
            ins.then_inc(K.full(("y", b)), 1)

        state_inputs(0)
        project("k", 4)
        tokens("av", 5)

        pe.wait_ge(K.sem["v_ready"], K.count("v_ready", l))
        pe.wait_ge(K.empty(("wT", 0)), K.drained_count(("wT", 0), l))
        for i in range(2):
            pe.wait_ge(K.empty(("mix", i)), K.empty_count(("mix", i), l))
            bank = pairs(K.bank(("mix", i)))
            for j in range(2):
                g = 2 * i + j
                for tt in range(TT):
                    out = bank[:, j, tt * P:(tt + 1) * P]
                    pe.matmul(out, K.v_ln[:, tt, g * P:(g + 1) * P], K.wT[:, g, :], start=True, stop=False)
                    ins = pe.matmul(out, K.ones[0:1, 0:P], K.sgu_bias[0:1, g * P:(g + 1) * P], start=False, stop=True)
            ins.then_inc(K.full(("mix", i)), 1)

        def attend_scores(h):
            if h == 0:
                for name in "qk":
                    for i in range(2):
                        pe.wait_ge(K.empty((name, i)), K.drained_count((name, i), l))
            rows, c = slice((h % 2) * HD, (h % 2) * HD + HD), h // 2
            pe.wait_ge(K.empty(("sc", h)), K.empty_count(("sc", h), l))
            bank = K.bank(("sc", h))
            pe.matmul(bank[:, 0:P], K.qT[rows, c, 0:P], K.kT[rows, c, 0:P], start=True, stop=True)
            pe.matmul(bank[:, P:3 * P], K.qT[rows, c, P:T], K.kT[rows, c, :], start=True, stop=True).then_inc(K.full(("sc", h)), 1)

        def attend_values(h):
            pe.wait_ge(K.sem["probs"], K.count("probs", l, h + 1))
            pe.wait_ge(K.empty(("pT", h)), K.empty_count(("pT", h), l))
            bank = K.bank(("pT", h))
            for i in range(3):
                ins = pe.transpose(bank[:, i * P:(i + 1) * P], K.prob[:, h % 2, i * P:(i + 1) * P], ident)
            ins.then_inc(K.full(("pT", h)), 1)

        def attend_out(hp):
            pe.wait_ge(K.empty(("o", hp)), K.empty_count(("o", hp), l))
            bank = K.bank(("o", hp))
            for h in (2 * hp, 2 * hp + 1):
                pe.wait_ge(K.empty(("pT", h)), K.drained_count(("pT", h), l))
                if h == 0:
                    for i in range(TT):
                        pe.wait_ge(K.empty(("av", i)), K.drained_count(("av", i), l))
                out = bank[(h % 2) * HD:(h % 2) * HD + HD, 0:T]
                pe.matmul(out, K.av[:, 0, h * HD:(h + 1) * HD], K.probT[:, h % 2, 0:T], start=True, stop=False)
                ins = pe.matmul(out[:, P:T], K.av[:, 1, h * HD:(h + 1) * HD], K.probT[:, h % 2, T:T + P], start=False, stop=True)
            ins.then_inc(K.full(("o", hp)), 1)

        def gates(n):
            pe.wait_ge(K.landed(("w_in", 6 + n // 2)), K.landed_count(("w_in", 6 + n // 2), l))
            w = K.weights(("w_in", 6 + n // 2), DC, BANK)
            channels(("gate",), n, w, K.xT, j0=2 * (n % 2))

        for n in range(HEADS):
            attend_scores(n)
            if n < 7:
                state_inputs(n + 1)
            for g in GATES_WITH[n]:
                gates(g)
            if n % 2 == 1:
                state_outputs(n // 2)
            attend_values(n)
            if n % 2 == 1:
                attend_out(n // 2)

        pe.wait_ge(K.sem["y_gelu"], K.count("y_gelu", l))
        pe.wait_ge(K.landed(("glu_w", 0)), K.landed_count(("glu_w", 0), l))
        w = K.weights(("glu_w", 0), WC, W5)
        for i in range(2):
            channels(("glu",), i, w, K.y_g, k=WC)
        for x, name in ((0, "w_a"), (2, "w_c"), (1, "w_b")):
            if x == 0:
                for i in range(2):
                    pe.wait_ge(K.empty(("mix", i)), K.drained_count(("mix", i), l))
            elif x == 2:
                pe.wait_ge(K.empty(("o", HEADS // 2 - 1)), K.drained_count(("o", HEADS // 2 - 1), l))
            else:
                pe.wait_ge(K.sem["glu_out"], K.count("glu_out", l))
            pe.wait_ge(K.landed((name, 0)), K.landed_count((name, 0), l))
            w = K.weights((name, 0), WC, D)
            for i in range(4):
                channels(("br", x), i, w, (K.uT, K.y_g, K.oT)[x], k=WC)
        pe.wait_ge(K.full(("br", 1, 3)), K.full_count(("br", 1, 3), l))
        pe.sem_inc(K.sem["params_free"], 1)
        pe.wait_ge(K.sem["merged"], K.count("merged", l))
        for hf in range(2):
            pe.wait_ge(K.landed(("w_out", hf)), K.landed_count(("w_out", hf), l))
            w = K.weights(("w_out", hf), DC, BANK)
            for tt in range(TT):
                pe.wait_ge(K.empty(("mo", tt, hf)), K.empty_count(("mo", tt, hf), l))
                bank = K.bank(("mo", tt, hf))
                for kc in range(DC):
                    ins = pe.matmul(bank, K.merged[:, kc, tt * P:(tt + 1) * P], w[:, kc, :], start=kc == 0, stop=kc == DC - 1)
                ins.then_inc(K.full(("mo", tt, hf)), 1)
        turn("x1", "x1T", K.x_tok)
        for q in range(4):
            pe.wait_ge(K.empty(("x1T", q)), K.drained_count(("x1T", q), l))
        for c in range(FFN_UNITS):
            pe.wait_ge(K.landed(("w13", c)), K.landed_count(("w13", c), l))
            both = K.weights(("w13", c), 2 * DC, FFN_COLS)
            for i, name in enumerate(("f1", "f3")):
                pe.wait_ge(K.empty((name, c)), K.empty_count((name, c), l))
                bank = pairs(K.bank((name, c)))
                for j in range(2):
                    for kc in range(DC):
                        ins = pe.matmul(bank[:, j, :], both[:, i * DC + kc, j * P:(j + 1) * P], K.xT[:, kc, :],
                                        start=kc == 0, stop=kc == DC - 1)
                ins.then_inc(K.full((name, c)), 1)
        pe.wait_ge(K.empty(("f2", tt, hf)), K.empty_count(("f2", tt, hf), l))
        banks = {(tt, hf): K.bank(("f2", tt, hf)) for tt in range(TT) for hf in range(2)}
        for u in range(W2_UNITS):
            n = min(W2_ROWS, FC - u * W2_ROWS)
            pe.wait_ge(K.landed(("w2", u)), K.landed_count(("w2", u), l))
            w = K.weights(("w2", u), n, D)
            for i in range(n):
                kc = u * W2_ROWS + i
                if kc % 2 == 0:
                    pe.wait_ge(K.empty(("f3", kc // 2)), K.drained_count(("f3", kc // 2), l))
                for (tt, hf), bank in banks.items():
                    ins = pe.matmul(bank, K.hT[:, kc, tt * P:(tt + 1) * P], w[:, i, hf * BANK:(hf + 1) * BANK],
                                    start=kc == 0, stop=kc == FC - 1)
                    if kc == FC - 1:
                        ins.then_inc(K.full(("f2", tt, hf)), 1)
            if u < W2_UNITS - 1:
                ins.then_inc(K.used_up(("w2", u)), 1)


def layer_scalar(act, K):
    with act.Fori(0, DEPTH) as l:

        def drain(key, dst, fn=ACT.Copy, src=lambda bank: bank, **kw):
            act.wait_ge(K.full(key), K.full_count(key, l))
            act.activation(dst, src(K.bank(key)), fn, **kw).then_inc(K.empty(key), 1)

        pairs = lambda bank: bank.rearrange("p (k n) -> p k n", k=2)
        for q in range(4):
            drain(("xT", q), K.xT[:, 2 * q:2 * q + 2, :], src=pairs)
        drain(("wT", 0), K.wT, src=lambda bank: bank.rearrange("p (g t) -> p g t", g=WC))
        blocks = lambda bank: bank.rearrange("p (b n) -> p b n", b=WC)
        drain(("CT", 0), K.cT_re, src=blocks)
        drain(("CT", 1), K.cT_im, src=blocks, scale=-1.0)
        act.wait_ge(K.empty(("vec", 0)), K.drained_count(("vec", 0), l))
        act.activation(K.sv[:, 0, :], K.vec[:, 64:64 + ST], ACT.Exp).then_inc(K.sem["ssm_dt"], 1)
        for i in range(2):
            drain(("ssm", i), K.zssm[:, 2 * i:2 * i + 2, :], src=pairs)
        act.wait_ge(K.sem["ssm_angle"], K.count("ssm_angle", l))
        act.activation(K.decay, K.sv[:, 1, :], ACT.Exp)
        act.activation(K.sv[:, 5, :], K.sv[:, 3, :], ACT.Sin, scale=TWO_PI)
        act.activation(K.sv[:, 6, :], K.sv[:, 4, :], ACT.Sin, scale=TWO_PI).then_inc(K.sem["ssm_trig"], 1)
        for tt in range(TT):
            drain(("v", tt), K.v_ln[:, tt, :], ACT.Gelu_apprx_tanh)
        for i in range(2):
            drain(("u", i), K.uT[:, 2 * i:2 * i + 2, :], ACT.Gelu_apprx_tanh, src=pairs)
        for i, dst in enumerate((K.bT_re, K.bT_im)):
            act.wait_ge(K.full(("BT", i)), K.full_count(("BT", i), l))
            bank = K.bank(("BT", i))
            for j in range(4):
                ins = act.activation(dst[32 * j:32 * j + 32, j, :], bank[32 * j:32 * j + 32, :], ACT.Copy)
            ins.then_inc(K.empty(("BT", i)), 1)
        act.wait_ge(K.sem["v_var"], K.count("v_var", l))
        act.activation(K.v_std, K.v_mv[:, :, 1], ACT.Sqrt).then_inc(K.sem["v_std"], 1)
        for i in range(2):
            drain(("q", i), K.qT[:, 2 * i:2 * i + 2, :], src=pairs)

        def rotation(n):
            act.wait_ge(K.sem["angle"], K.count("angle", l, n + 1))
            if n >= 2:
                act.wait_ge(K.sem["h_ready"], K.count("h_ready", l, n - 1))
            act.activation(K.sin[:, n % 2, :], K.angle, ACT.Sin, scale=TWO_PI)
            act.activation(K.angle, K.angle, ACT.Abs).then_inc(K.link_act.sem, 1)
            act.wait_ge(K.link_act.sem, K.link_act.count())
            act.activation(K.cos[:, n % 2, :], K.angle, ACT.Sin, scale=-TWO_PI, bias=K.half_pi).then_inc(K.sem["cos_sin"], 1)

        K.link_act = Chain(K.act_done, 0, l, ACT_LINKS)
        rotation(0)
        rotation(1)
        for i in range(2):
            drain(("k", i), K.kT[:, 2 * i:2 * i + 2, :], src=pairs)
        for tt in range(TT):
            drain(("av", tt), K.av[:, tt, :])
        for n in range(HEADS):
            act.wait_ge(K.sem["neg_max"], K.count("neg_max", l, n + 1))
            if n >= 2:
                act.wait_ge(K.empty(("pT", n - 2)), K.drained_count(("pT", n - 2), l))
            act.activation(K.prob[:, n % 2, 0:P], K.score[:, n % 2, 0:P], ACT.Exp, bias=K.negmax[:, n % 2, 0:1],
                           scale=HD ** -0.5, accum_out=K.rowsum[:, n % 2, 0:1])
            act.activation(K.prob[:, n % 2, P:3 * P], K.score[:, n % 2, P:3 * P], ACT.Exp,
                                    bias=K.negmax[:, n % 2, 1:2], scale=HD ** -0.5,
                                    accum_out=K.rowsum[:, n % 2, 1:2]).then_inc(K.sem["exped"], 1)
            for g in GATES_WITH[n]:
                drain(("gate", g), K.gates[:, 2 * g:2 * g + 2, :], ACT.Sigmoid, src=pairs)
            if n < 6:
                rotation(n + 2)
            drain(("pT", n), K.probT[:, n % 2, :], src=lambda bank: bank[:, 0:3 * P])
            if n % 2 == 1:
                drain(("o", n // 2), K.oT[:, n // 2, :], src=lambda bank: bank[:, 0:T])
                act.wait_ge(K.empty(("y", n // 2)), K.drained_count(("y", n // 2), l))
                act.activation(K.y_g[:, n // 2, :], K.zssm[:, n // 2, :], ACT.Gelu_apprx_tanh).then_inc(K.sem["y_gelu"], 1)
        K.link_act.end(DEPTH)
        act.wait_ge(K.sem["y_gelu"], K.count("y_gelu", l))
        for i in range(2):
            act.wait_ge(K.full(("glu", i)), K.full_count(("glu", i), l))
            bank = pairs(K.bank(("glu", i)))
            for j in range(2):
                c = 2 * i + j
                ins = act.activation(K.zssm[:, c, :], bank[:, j, :], ACT.Sigmoid, bias=K.vec[:, 96 + WC + c:97 + WC + c])
            ins.then_inc(K.empty(("glu", i)), 1)
        for tt in range(TT):
            act.wait_ge(K.sem["x1_var"], K.count("x1_var", l, tt + 1))
            act.activation(K.x_std[:, tt:tt + 1], K.x_mv[:, tt, 1:2], ACT.Sqrt).then_inc(K.sem["x1_std"], 1)
        for q in range(4):
            drain(("x1T", q), K.xT[:, 2 * q:2 * q + 2, :], src=pairs)
        for c in range(FFN_UNITS):
            if c >= 2:
                act.wait_ge(K.empty(("f3", c - 2)), K.drained_count(("f3", c - 2), l))
            drain(("f1", c), K.silu[:, c % 2, :], ACT.Silu)
        for tt in range(TT):
            act.wait_ge(K.sem["x2_var"], K.count("x2_var", l, tt + 1))
            act.activation(K.x_std[:, tt:tt + 1], K.x_mv[:, tt, 1:2], ACT.Sqrt).then_inc(K.sem["x2_std"], 1)


def layer_gpsimd(pool, K):
    with pool.Fori(0, DEPTH) as l:
        link = Chain(K.pool_done, 0, l, POOL_LINKS)
        pool.wait_ge(K.sem["dma_params"], K.count("dma_params", l))
        pool.sem_inc(link.sem, 1)
        link.count()
        pool.affine_select(out=K.w_nat, in_=K.w_nat, compare_op=ALU.is_ge, fill=0.0, base=0,
                                    pattern=[[0, WC], [-1, P]], channel_multiplier=1).then_inc(K.sem["tril"], 1)

        def angles(n):
            if n:
                pool.wait_ge(K.sem["cos_sin"], K.count("cos_sin", l, n))
            out = K.angle.rearrange("p (j t) -> p j t", j=2)
            pool.tensor_tensor(out, K.token.unsqueeze(1).broadcast_to([P, 2, T]),
                                    K.sv[:, 3, 2 * n:2 * n + 2].unsqueeze(2).broadcast_to([P, 2, T]), ALU.mult).then_inc(link.sem, 1)
            pool.wait_ge(link.sem, link.count())
            pool.sem_inc(link.sem, 1)
            link.count()
            pool.tensor_scalar(K.pool_tmp[:, 0, :], K.angle, MAGIC, -MAGIC, ALU.add, ALU.add).then_inc(link.sem, 1)
            pool.wait_ge(link.sem, link.count())
            pool.tensor_tensor(K.angle, K.angle, K.pool_tmp[:, 0, :], ALU.subtract).then_inc(K.sem["angle"], 1)
            pool.wait_ge(K.sem["angle"], K.count("angle", l, n + 1))

        def turn_back(n):
            pool.wait_ge(K.sem["scanned"], K.count("scanned", l, n + 1))
            if n >= 2:
                pool.wait_ge(K.full(("y", (n - 2) // 2)), K.full_count(("y", (n - 2) // 2), l))
            c, s, t = K.cos[:, n % 2, :], K.sin[:, n % 2, :], K.pool_tmp
            pool.tensor_tensor(t[:, 0, :], K.g_re[:, n % 2, :], c, ALU.mult).then_inc(link.sem, 1)
            pool.wait_ge(link.sem, link.count())
            pool.tensor_tensor(t[:, 1, :], K.g_im[:, n % 2, :], s, ALU.mult).then_inc(link.sem, 1)
            pool.wait_ge(link.sem, link.count())
            pool.tensor_tensor(K.h_re[:, n % 2, :], t[:, 0, :], t[:, 1, :], ALU.subtract).then_inc(link.sem, 1)
            pool.wait_ge(link.sem, link.count())
            pool.tensor_tensor(t[:, 0, :], K.g_re[:, n % 2, :], s, ALU.mult).then_inc(link.sem, 1)
            pool.wait_ge(link.sem, link.count())
            pool.tensor_tensor(t[:, 1, :], K.g_im[:, n % 2, :], c, ALU.mult).then_inc(link.sem, 1)
            pool.wait_ge(link.sem, link.count())
            pool.tensor_tensor(K.h_im[:, n % 2, :], t[:, 0, :], t[:, 1, :], ALU.add).then_inc(K.sem["h_ready"], 1)
            pool.wait_ge(K.sem["h_ready"], K.count("h_ready", l, n + 1))

        pool.wait_ge(K.sem["ssm_angle"], K.count("ssm_angle", l))
        angles(0)
        angles(1)
        pool.wait_ge(K.sem["v_norm"], K.count("v_norm", l))
        for tt in range(TT):
            pool.tensor_tensor(K.v_ln[:, tt, :], K.v_ln[:, tt, :], K.v_gain, ALU.mult).then_inc(link.sem, 1)
            pool.wait_ge(link.sem, link.count())
            ins = pool.tensor_tensor(K.v_ln[:, tt, :], K.v_ln[:, tt, :], K.v_bias, ALU.add)
        ins.then_inc(K.sem["v_ready"], 1)
        for n in range(8):
            if n < 6:
                angles(n + 2)
            turn_back(n)
        link.end(DEPTH)


def layer_vector(dve, K):
    with dve.Fori(0, DEPTH) as l:
        link = Chain(K.dve_done, 0, l, 0)
        link.per = K.dve_links
        V, sv = K.vec, K.sv
        tt_op, ts_op = dve.tensor_tensor, dve.tensor_scalar

        dve.wait_ge(K.sem["dma_params"], K.count("dma_params", l))
        dve.tensor_copy(K.vrows[64:64 + ST, :].rearrange("t (g p) -> t g p", g=2),
                                 K.dtrow[64:64 + ST, :].unsqueeze(2).broadcast_to([ST, 2, 64])).then_inc(K.sem["dt_row"], 1)
        dve.wait_ge(K.full(("vec", 0)), K.full_count(("vec", 0), l))
        dve.tensor_copy(V, K.bank(("vec", 0))[:, 0:P]).then_inc(K.empty(("vec", 0)), 1)
        dve.wait_ge(K.empty(("vec", 0)), K.drained_count(("vec", 0), l))
        re, im = V[:, 0:ST], V[:, 32:32 + ST]
        dve.wait_ge(K.sem["ssm_dt"], K.count("ssm_dt", l))
        tt_op(sv[:, 1, :], re, sv[:, 0, :], ALU.mult).then_inc(link.sem, 1)
        dve.wait_ge(link.sem, link.count())
        tt_op(sv[:, 2, :], im, sv[:, 0, :], ALU.mult).then_inc(link.sem, 1)
        dve.wait_ge(link.sem, link.count())
        ts_op(sv[:, 2, :], sv[:, 2, :], 1 / (2 * math.pi), None, ALU.mult).then_inc(link.sem, 1)
        dve.wait_ge(link.sem, link.count())
        ts_op(sv[:, 7, :], sv[:, 2, :], MAGIC, -MAGIC, ALU.add, ALU.add).then_inc(link.sem, 1)
        dve.wait_ge(link.sem, link.count())
        tt_op(sv[:, 3, :], sv[:, 2, :], sv[:, 7, :], ALU.subtract).then_inc(link.sem, 1)
        dve.wait_ge(link.sem, link.count())
        ts_op(sv[:, 4, :], sv[:, 3, :], 0.25, None, ALU.add).then_inc(link.sem, 1)
        dve.wait_ge(link.sem, link.count())
        ts_op(sv[:, 7, :], sv[:, 4, :], MAGIC, -MAGIC, ALU.add, ALU.add).then_inc(link.sem, 1)
        dve.wait_ge(link.sem, link.count())
        tt_op(sv[:, 4, :], sv[:, 4, :], sv[:, 7, :], ALU.subtract).then_inc(K.sem["ssm_angle"], 1)
        dve.wait_ge(K.sem["ssm_trig"], K.count("ssm_trig", l))
        tt_op(sv[:, 6, :], K.decay, sv[:, 6, :], ALU.mult).then_inc(link.sem, 1)
        dve.wait_ge(link.sem, link.count())
        ts_op(sv[:, 6, :], sv[:, 6, :], -1.0, None, ALU.add).then_inc(link.sem, 1)
        dve.wait_ge(link.sem, link.count())
        tt_op(sv[:, 5, :], K.decay, sv[:, 5, :], ALU.mult).then_inc(link.sem, 1)
        dve.wait_ge(link.sem, link.count())
        tt_op(sv[:, 7, :], re, re, ALU.mult).then_inc(link.sem, 1)
        dve.wait_ge(link.sem, link.count())
        tt_op(sv[:, 8, :], im, im, ALU.mult).then_inc(link.sem, 1)
        dve.wait_ge(link.sem, link.count())
        tt_op(sv[:, 7, :], sv[:, 7, :], sv[:, 8, :], ALU.add).then_inc(link.sem, 1)
        dve.wait_ge(link.sem, link.count())
        dve.reciprocal(sv[:, 7, :], sv[:, 7, :]).then_inc(link.sem, 1)
        dve.wait_ge(link.sem, link.count())
        tt_op(sv[:, 8, :], sv[:, 6, :], re, ALU.mult).then_inc(link.sem, 1)
        dve.wait_ge(link.sem, link.count())
        tt_op(sv[:, 9, :], sv[:, 5, :], im, ALU.mult).then_inc(link.sem, 1)
        dve.wait_ge(link.sem, link.count())
        tt_op(sv[:, 8, :], sv[:, 8, :], sv[:, 9, :], ALU.add).then_inc(link.sem, 1)
        dve.wait_ge(link.sem, link.count())
        tt_op(sv[:, 8, :], sv[:, 8, :], sv[:, 7, :], ALU.mult).then_inc(link.sem, 1)
        dve.wait_ge(link.sem, link.count())
        tt_op(sv[:, 9, :], sv[:, 5, :], re, ALU.mult).then_inc(link.sem, 1)
        dve.wait_ge(link.sem, link.count())
        tt_op(sv[:, 10, :], sv[:, 6, :], im, ALU.mult).then_inc(link.sem, 1)
        dve.wait_ge(link.sem, link.count())
        tt_op(sv[:, 9, :], sv[:, 9, :], sv[:, 10, :], ALU.subtract).then_inc(link.sem, 1)
        dve.wait_ge(link.sem, link.count())
        tt_op(sv[:, 9, :], sv[:, 9, :], sv[:, 7, :], ALU.mult).then_inc(link.sem, 1)
        dve.wait_ge(link.sem, link.count())
        cr, ci = (sv[:, i, :].unsqueeze(2).broadcast_to([P, ST, 32]) for i in (8, 9))
        tmp = K.dve_tmp[:, 0, :].rearrange("p (t h) -> p t h", h=32)
        tt_op(K.bbar_re, K.b_nat_re, cr, ALU.mult).then_inc(link.sem, 1)
        dve.wait_ge(link.sem, link.count())
        tt_op(tmp, K.b_nat_im, ci, ALU.mult).then_inc(link.sem, 1)
        dve.wait_ge(link.sem, link.count())
        tt_op(K.bbar_re, K.bbar_re, tmp, ALU.subtract).then_inc(link.sem, 1)
        dve.wait_ge(link.sem, link.count())
        tt_op(K.bbar_im, K.b_nat_im, cr, ALU.mult).then_inc(link.sem, 1)
        dve.wait_ge(link.sem, link.count())
        tt_op(tmp, K.b_nat_re, ci, ALU.mult).then_inc(link.sem, 1)
        dve.wait_ge(link.sem, link.count())
        tt_op(K.bbar_im, K.bbar_im, tmp, ALU.add).then_inc(K.sem["ssm_bbar"], 1)

        def stats(src, mv, st, n):
            for i in range(n):
                dve.bn_stats(st[:, i, :], src[:, i * BANK:(i + 1) * BANK]).then_inc(link.sem, 1)
                dve.wait_ge(link.sem, link.count())
            dve.sem_inc(link.sem, 1)
            link.count()
            dve.bn_aggr(mv, st[:, 0:n, :].rearrange("p a b -> p (a b)")).then_inc(link.sem, 1)
            dve.wait_ge(link.sem, link.count())

        for tt in range(TT):
            dve.wait_ge(K.empty(("v", tt)), K.drained_count(("v", tt), l))
            stats(K.v_ln[:, tt, :], K.v_mv[:, tt, :], K.bn, 1)
        ts_op(K.v_mv[:, :, 1], K.v_mv[:, :, 1], LN_EPS, None, ALU.add).then_inc(K.sem["v_var"], 1)

        def scan(n):
            dve.wait_ge(K.sem["cos_sin"], K.count("cos_sin", l, n + 1))
            c, s, t = K.cos[:, n % 2, :], K.sin[:, n % 2, :], K.dve_tmp
            dve.wait_ge(K.full(("bu", n, 0)), K.full_count(("bu", n, 0), l))
            dve.wait_ge(K.full(("bu", n, 1)), K.full_count(("bu", n, 1), l))
            b_re, b_im = K.bank(("bu", n, 0)), K.bank(("bu", n, 1))
            tt_op(t[:, 0, :], b_re, c, ALU.mult).then_inc(link.sem, 1)
            dve.wait_ge(link.sem, link.count())
            tt_op(t[:, 1, :], b_im, s, ALU.mult).then_inc(link.sem, 1)
            dve.wait_ge(link.sem, link.count())
            tt_op(t[:, 3, :], b_re, s, ALU.mult).then_inc(K.empty(("bu", n, 0)), 1)
            tt_op(t[:, 2, :], b_im, c, ALU.mult).then_inc(K.empty(("bu", n, 1)), 1)
            tt_op(t[:, 0, :], t[:, 0, :], t[:, 1, :], ALU.add).then_inc(link.sem, 1)
            dve.wait_ge(link.sem, link.count())
            for i in range(2):
                dve.wait_ge(K.empty(("bu", n, i)), K.drained_count(("bu", n, i), l))
            tt_op(t[:, 2, :], t[:, 2, :], t[:, 3, :], ALU.subtract).then_inc(link.sem, 1)
            dve.wait_ge(link.sem, link.count())
            if n >= 2:
                dve.wait_ge(K.sem["h_ready"], K.count("h_ready", l, n - 1))
            for j in range(2):
                r = K.decay[:, 2 * n + j:2 * n + j + 1].broadcast_to([P, T])
                cols = slice(j * T, (j + 1) * T)
                dve.tensor_tensor_scan(K.g_re[:, n % 2, cols], r, t[:, 0, cols], 0.0, ALU.mult, ALU.add)
                ins = dve.tensor_tensor_scan(K.g_im[:, n % 2, cols], r, t[:, 2, cols], 0.0, ALU.mult, ALU.add)
            ins.then_inc(K.sem["scanned"], 1)

        scan(0)
        dve.wait_ge(K.sem["v_std"], K.count("v_std", l))
        dve.reciprocal(K.v_std, K.v_std).then_inc(link.sem, 1)
        dve.wait_ge(link.sem, link.count())
        for tt in range(TT):
            ins = ts_op(K.v_ln[:, tt, :], K.v_ln[:, tt, :], K.v_mv[:, tt, 0:1], K.v_std[:, tt:tt + 1], ALU.subtract, ALU.mult)
        ins.then_inc(K.sem["v_norm"], 1)
        for i in range(2):
            dve.wait_ge(K.empty(("u", i)), K.drained_count(("u", i), l))
            dve.wait_ge(K.full(("mix", i)), K.full_count(("mix", i), l))
            bank = K.bank(("mix", i)).rearrange("p (k n) -> p k n", k=2)
            tt_op(K.uT[:, 2 * i:2 * i + 2, :], K.uT[:, 2 * i:2 * i + 2, :], bank, ALU.mult).then_inc(K.empty(("mix", i)), 1)
        for n in range(HEADS):
            b = n % 2
            dve.wait_ge(K.full(("sc", n)), K.full_count(("sc", n), l))
            bank = K.bank(("sc", n))
            if n >= 2:
                dve.wait_ge(K.sem["exped"], K.count("exped", l, n - 1))
            slope = 2.0 ** (-8.0 * (n + 1) / HEADS)
            dve.scalar_tensor_tensor(out=K.score[:, b, :], in0=K.distance, scalar=slope * HD ** 0.5,
                                               in1=bank[:, 0:3 * P], op0=ALU.mult, op1=ALU.add).then_inc(K.empty(("sc", n)), 1)
            dve.wait_ge(K.empty(("sc", n)), K.drained_count(("sc", n), l))
            dve.tensor_reduce(K.negmax[:, b, 0:1], K.score[:, b, 0:P], AX_X, ALU.max).then_inc(link.sem, 1)
            dve.wait_ge(link.sem, link.count())
            dve.tensor_reduce(K.negmax[:, b, 1:2], K.score[:, b, P:3 * P], AX_X, ALU.max).then_inc(link.sem, 1)
            dve.wait_ge(link.sem, link.count())
            ts_op(K.negmax[:, b, :], K.negmax[:, b, :], -HD ** -0.5, None, ALU.mult).then_inc(K.sem["neg_max"], 1)
            if n < 7:
                scan(n + 1)
            dve.wait_ge(K.sem["exped"], K.count("exped", l, n + 1))
            dve.reciprocal(K.rowsum[:, b, :], K.rowsum[:, b, :]).then_inc(link.sem, 1)
            dve.wait_ge(link.sem, link.count())
            ts_op(K.prob[:, b, 0:P], K.prob[:, b, 0:P], K.rowsum[:, b, 0:1], None, ALU.mult)
            ts_op(K.prob[:, b, P:3 * P], K.prob[:, b, P:3 * P], K.rowsum[:, b, 1:2], None, ALU.mult).then_inc(K.sem["probs"], 1)
            if n % 2 == 1:
                c = n // 2
                dve.wait_ge(K.full(("y", c)), K.full_count(("y", c), l))
                dve.scalar_tensor_tensor(out=K.zssm[:, c, :], in0=K.zssm[:, c, :], scalar=V[:, 96 + c:97 + c],
                                                   in1=K.bank(("y", c))[:, 0:T], op0=ALU.mult, op1=ALU.add).then_inc(K.empty(("y", c)), 1)
        dve.wait_ge(K.sem["y_gelu"], K.count("y_gelu", l))
        dve.wait_ge(K.empty(("glu", 0)), K.drained_count(("glu", 0), l))
        dve.wait_ge(K.empty(("glu", 1)), K.drained_count(("glu", 1), l))
        tt_op(K.y_g, K.y_g, K.zssm, ALU.mult).then_inc(K.sem["glu_out"], 1)
        pairs = lambda bank: bank.rearrange("p (k n) -> p k n", k=2)
        for x in (0, 2, 1):
            for i in range(4):
                dve.wait_ge(K.empty(("gate", 4 * x + i)), K.drained_count(("gate", 4 * x + i), l))
                dve.wait_ge(K.full(("br", x, i)), K.full_count(("br", x, i), l))
                bank = pairs(K.bank(("br", x, i)))
                m = K.merged[:, 2 * i:2 * i + 2, :]
                g = K.gates[:, 8 * x + 2 * i:8 * x + 2 * i + 2, :]
                if x == 0:
                    tt_op(m, g, bank, ALU.mult).then_inc(K.empty(("br", x, i)), 1)
                    continue
                part = pairs(K.dve_tmp[:, i % 2, :])
                tt_op(part, g, bank, ALU.mult).then_inc(K.empty(("br", x, i)), 1)
                dve.wait_ge(K.empty(("br", x, i)), K.drained_count(("br", x, i), l))
                ins = tt_op(m, m, part, ALU.add)
                if x == 2:
                    ins.then_inc(link.sem, 1)
                    dve.wait_ge(link.sem, link.count())
                else:
                    ins.then_inc(K.sem["merged"], 1)

        def norm(name, key, row, last):
            for tt in range(TT):
                for hf in range(2):
                    part = K.x_tok[:, tt, hf * BANK:(hf + 1) * BANK]
                    dve.wait_ge(K.full((key, tt, hf)), K.full_count((key, tt, hf), l))
                    dve.scalar_tensor_tensor(out=part, in0=part, scalar=DN_ALPHA, in1=K.bank((key, tt, hf)),
                                                       op0=ALU.mult, op1=ALU.add).then_inc(K.empty((key, tt, hf)), 1)
                    dve.wait_ge(K.empty((key, tt, hf)), K.drained_count((key, tt, hf), l))
                stats(K.x_tok[:, tt, :], K.x_mv[:, tt, :], K.bn, 2)
                ts_op(K.x_mv[:, tt, 1:2], K.x_mv[:, tt, 1:2], LN_EPS, None, ALU.add).then_inc(K.sem[name + "_var"], 1)
            dve.wait_ge(K.sem["dma_ln"], K.count("dma_ln", l))
            for tt in range(TT):
                dve.wait_ge(K.sem[name + "_std"], K.count(name + "_std", l, tt + 1))
                x = K.x_tok[:, tt, :]
                dve.reciprocal(K.x_std[:, tt:tt + 1], K.x_std[:, tt:tt + 1]).then_inc(link.sem, 1)
                dve.wait_ge(link.sem, link.count())
                ts_op(x, x, K.x_mv[:, tt, 0:1], K.x_std[:, tt:tt + 1], ALU.subtract, ALU.mult).then_inc(link.sem, 1)
                dve.wait_ge(link.sem, link.count())
                tt_op(x, x, K.ln_rows[:, row, :], ALU.mult).then_inc(link.sem, 1)
                dve.wait_ge(link.sem, link.count())
                ins = tt_op(x, x, K.ln_rows[:, row + 1, :], ALU.add)
                if last is None:
                    ins.then_inc(K.sem[name], 1)
                elif tt == TT - 1:
                    ins.then_inc(K.sem[last], 1)
                else:
                    ins.then_inc(link.sem, 1)
                    dve.wait_ge(link.sem, link.count())

        norm("x1", "mo", 0, None)
        for c in range(FFN_UNITS):
            dve.wait_ge(K.empty(("f1", c)), K.drained_count(("f1", c), l))
            dve.wait_ge(K.full(("f3", c)), K.full_count(("f3", c), l))
            tt_op(K.hT[:, 2 * c:2 * c + 2, :], pairs(K.silu[:, c % 2, :]), pairs(K.bank(("f3", c))), ALU.mult).then_inc(K.empty(("f3", c)), 1)
        norm("x2", "f2", 2, "x_in")
        link.end(DEPTH)



S_ALL = 2 * T
SB = S_ALL // P
HH = 8
ZS = 2
Z0 = 32
CH = 64
HP = HH // 2
ALPHA_2 = 2.0 ** 0.25
LN_EPS_2 = 1e-6
GN_EPS = 64e-5
DECAY_SCALE = math.exp(-0.5)
EXPERTS, GROUPS_E, PER_GROUP, D_EXPERT = 32, 4, 8, 512
EC = D_EXPERT // P
IN_2 = 3936
LAST_COLS = IN_2 - 7 * BANK
CONV_CHUNKS = 20
VROWS = dict(b_ada=(0, 48), m_norm_w=(48, 4), r_w0=(52, 8), r_a0=(60, 4), r_kk=(64, 4), r_ka=(68, 4), r_bonus=(72, 4),
             r_norm_w=(76, 4), r_norm_b=(80, 4), c=(84, 8), c_ctx=(92, 8))
BIG = 1e30


def mid_units():
    return [("ada", c) for c in (0, 1, 2, 3, 6, 7, 8, 9)] + [("w2in", c) for c in (7, 3, 4, 2, 1, 0, 5, 6)]


def mid_groups():
    keys = [("bvec", 0)]
    for m in range(2):
        keys += [("mod_row", m, i) for i in range(4)] + [("mod", m)]
    keys += [("hT", s, q) for s in range(2) for q in range(4)]
    keys += [("lif", 0), ("lw", 0), ("la", 0), ("lg", 0)]
    keys += [("rk", c) for c in range(4)] + [("al", c) for c in range(4)]
    keys += [("wl", z, c) for z in range(ZS) for c in range(4)] + [("gl", i) for i in range(2)]
    keys += [("rv", c) for c in range(4)] + [("rr", i) for i in range(2)] + [("mk", c) for c in range(4)]
    keys += [("ss", c) for c in range(4)]
    keys += [("mq", i) for i in range(2)] + [("mv", i) for i in range(SB)] + [("mo2", i) for i in range(2)]
    keys += [("bs", i) for i in range(2)] + [("gT", 0)]
    for h in range(HH):
        keys += [("bG", h), ("qk", h, 0), ("qk", h, 1)]
        if h % 2:
            keys += [("em", h // 2), ("num", h // 2), ("den", h // 2)]
    return keys + [(k, hp) for k in ("hm", "hv") for hp in range(HP)]


def mid_closes():
    closes = {("mod_row", m, i): ("ada", 6 * m + i) for m in range(2) for i in range(4)} | {("lg", 0): ("w2in", 7)}
    return closes | {("rk", 3): ("w2in", 3), ("rv", 3): ("w2in", 4), ("rr", 1): ("w2in", 2), ("mk", 3): ("w2in", 1),
                     ("mq", 1): ("w2in", 0), ("mv", 3): ("w2in", 5), ("mo2", 1): ("w2in", 6)}


LEVELS = 6


def chunk_groups(ph, lat):
    keys = []
    for z in range(ZS):
        keys += [(ph, "mT", z, i) for i in range(2)] + [(ph, "nT", z, i) for i in range(2)]
        keys += [(ph, "m", z)] + [(ph, k, z) for k in ("bt", "kt", "vt")]
    for n in range(1, LEVELS + 1):
        for z in range(ZS):
            if n > 1:
                keys += [(ph, "inv", n, z)]
            if n < LEVELS - 1:
                keys += [(ph, "pow", n, z)]
            if n < LEVELS:
                keys += [(ph, "powT", n, z)]
    keys += [(ph, k, z) for k in ("a1", "u") + (("y",) if lat else ()) + ("s",) for z in range(ZS)]
    return keys + [None] * (-len(keys) % BANKS)


def tail_units():
    return [("ada", 4), ("ada", 5), ("wo2", 0), ("wo2", 1), ("ada", 10), ("ada", 11)]


def tail_groups():
    keys = [(k, hp) for k in ("ym", "yv") for hp in range(HP)] + [("g1", i) for i in range(2)]
    keys += [("out2", tt, hf) for hf in range(2) for tt in range(TT)] + [("h2T", q) for q in range(4)]
    keys += [("rt", tt) for tt in range(TT)] + [("h2", tt, hf) for tt in range(TT) for hf in range(2)]
    return keys + [("g2", i) for i in range(2)] + [("pos", tt) for tt in range(TT)]


def tail_closes():
    return {("g1", i): ("ada", 4 + i) for i in range(2)} | {("g2", i): ("ada", 10 + i) for i in range(2)} | {
        ("out2", 1, i): ("wo2", i) for i in range(2)}


PLACES = 64
TOP = 2
BLOCKS = (TOP * T + EXPERTS * (PLACES - 1)) // PLACES
PAIRS = -(-BLOCKS // 2)


def pair_units():
    return [(kind, j) for j in range(2) for kind in ("pair_gate", "pair_up", "pair_down")]


def pair_groups():
    keys = [("xg", 0), ("xg", 1), ("pgate", 0), ("pup", 0), ("putT", 0), ("pdown", 0), ("pdown", 1), ("pgate", 1), ("pup", 1)]
    keys += [("put", tt, hf) for hf in range(2) for tt in range(TT)]
    return keys + [None] * (-len(keys) % BANKS)


def pair_closes():
    return {("pgate", j): ("pair_gate", j) for j in range(2)} | {("pup", j): ("pair_up", j) for j in range(2)} | {
        ("pdown", 1): ("pair_down", 1)}


MID_EVENTS = dict(
    dma_vec=18, dma_ctx=1, dma_lora=3, silu_c=1, mod=2, nrm_var=2, nrm_std=2, nrm=2, gate_x=1, gate_ln=1, gates_ready=1,
    rk_center=4, rv_center=4, rr_center=4, mk_center=4, mq_center=4, pick=1, gate_w=1, h_m_done=1,
    conv_mk=4, conv_mq=4, kap_sq=4, ss_root=4, kh=4, bonus_in=2, cum=8,
    expo_in=16, expo=16, masked=16, weights_m=16, h_m=4, hm_sq=4, hm_var=4, hm_std=4,
    hm_c=4, zeros=1, rows_clear=1, km=1, qm=1,
)
CHUNK_EVENTS = {f"{ph}_{name}": ZS for ph in ("ctx", "lat") for name in ("decay", "hats", "v_blocks", "inv_start", "sum")}
TAIL_EVENTS = dict(
    chunk_zeros=2, y_ready=4, y_c=4, y_sq=4, y_var=4, y_std=4, mixed_r=4, c_rows=1, dma_tail=9,
    x3_var=2, x3_std=2, x3=2, x4_var=2, x4_std=2, x4=2, rt_exp=2, rt_e2=2, route=2, acc_zero=1,
    planned=1, selected=1,
    x5_var=2, x5_std=2, x5=1,
)


def mid_sync(sp, K, A):
    rows = lambda a: a[0].rearrange("(k p) n -> p k n", p=P)
    for c in (0, 1, 2):
        sp.wait_ge(K.used_up(("ada", c)), K.free_count(("ada", c)))
        weights = rows(A["w_ada_2"])[:, :, c * BANK:(c + 1) * BANK]
        sp.dma_start(K.slot_like(("ada", c), weights), weights).then_inc(K.landed(("ada", c)), 16)
    sp.wait_ge(K.sem["x_in"], K.count("x_in", DEPTH))
    sp.wait_ge(K.sem["rows_clear"], K.count("rows_clear"))
    def put(dst, src):
        sp.dma_start(dst, src).then_inc(K.sem["dma_vec"], 16)

    def vrow(name, src):
        lo, n = VROWS[name]
        put(K.vrows2[lo:lo + n, :], src.rearrange("a (k p) -> (a k) p", p=P))

    vrow("c", A["c_2"])
    vrow("c_ctx", A["c_ctx_2"].unsqueeze(0))
    for name, a in (("b_ada", A["b_ada_2"]), ("m_norm_w", A["m_norm_w_2"]), ("r_w0", A["r_w0_2"][0]), ("r_a0", A["r_a0_2"]),
                    ("r_kk", A["r_kk_2"]), ("r_ka", A["r_ka_2"]), ("r_bonus", A["r_bonus_2"][0]), ("r_norm_w", A["r_norm_w_2"]),
                    ("r_norm_b", A["r_norm_b_2"])):
        if name == "r_bonus":
            a = a.rearrange("h d -> (h d)").unsqueeze(0)
        vrow(name, a)
    taps = A["conv_w_2"][0].rearrange("a b (c p) -> (a b c) p", p=P)
    put(K.crows[:, 0, :], taps[0:P, :])
    put(K.crows[0:9 * CONV_CHUNKS - P, 1, :], taps[P:9 * CONV_CHUNKS, :])
    for z in range(ZS):
        put(K.bias_i[Z0 * z:Z0 * z + HH, :], A["m_bias_i_2"][0, z].unsqueeze(1))
        put(K.bias_f[2 * Z0 + Z0 * z:2 * Z0 + Z0 * z + HH, :], A["m_bias_f_2"][0, z].unsqueeze(1))
    put(K.rt_bias[0:1, 0:GROUPS_E], A["rt_g_b_2"])
    sp.dma_start(K.nrm[:, 0], A["ctx_2"][0].rearrange("(a p) d -> p a d", p=P)).then_inc(K.sem["dma_ctx"], 16)
    sp.dma_start(K.wB, A["r_wB_2"][0].rearrange("z r n -> (z r) n")).then_inc(K.sem["dma_lora"], 16)
    sp.dma_start(K.aB[0:64, :], A["r_aB_2"][0]).then_inc(K.sem["dma_lora"], 16)
    sp.dma_start(K.gB, A["r_gB_2"][0]).then_inc(K.sem["dma_lora"], 16)
    for kind, c in mid_units()[3:]:
        if kind == "ada":
            sp.wait_ge(K.used_up((kind, c)), K.free_count((kind, c)))
            weights = rows(A["w_ada_2"])[:, :, c * BANK:(c + 1) * BANK]
            sp.dma_start(K.slot_like((kind, c), weights), weights).then_inc(K.landed((kind, c)), 16)
        else:
            sp.wait_ge(K.used_up((kind, c)), K.free_count((kind, c)))
            weights = rows(A["w_in_2"])[:, :, c * BANK:min((c + 1) * BANK, IN_2)]
            sp.dma_start(K.slot_like((kind, c), weights), weights).then_inc(K.landed((kind, c)), 16)


def mid_tensor(pe, K):
    ident = K.ident

    def product(out, pairs_, last=None):
        for i, (a, b) in enumerate(pairs_):
            ins = pe.matmul(out, a, b, start=i == 0, stop=i == len(pairs_) - 1)
        if last:
            ins.then_inc(K.full(last), 1)
        return ins

    pe.wait_ge(K.sem["dma_vec"], K.count("dma_vec"))
    pe.wait_ge(K.sem["zeros"], K.count("zeros"))
    pe.wait_ge(K.empty(("bvec", 0)), K.empty_count(("bvec", 0)))
    bank = K.bank(("bvec", 0))
    pe.transpose(bank[:, 0:P], K.vrows2, ident)
    pe.transpose(bank[:, P:2 * P], K.crows[:, 0, :], ident)
    n = 9 * CONV_CHUNKS - P
    pe.transpose(bank[:, 2 * P:2 * P + n], K.crows[0:n, 1, :], ident[0:n, 0:n]).then_inc(K.full(("bvec", 0)), 1)
    pe.wait_ge(K.sem["silu_c"], K.count("silu_c"))
    for m in range(2):
        for i in range(4):
            unit = ("ada", 6 * m + i)
            pe.wait_ge(K.landed(unit), K.landed_count(unit))
            w = K.weights(unit, DC, BANK)
            pe.wait_ge(K.empty(("mod_row", m, i)), K.empty_count(("mod_row", m, i)))
            rows = K.bank(("mod_row", m, i))[0:2, :]
            for kc in range(DC):
                ins = pe.matmul(rows, K.c_col[:, kc, :], w[:, kc, :], start=kc == 0, stop=kc == DC - 1)
            ins.then_inc(K.full(("mod_row", m, i)), 1)
        for i in range(4):
            pe.wait_ge(K.empty(("mod_row", m, i)), K.drained_count(("mod_row", m, i)))
        pe.wait_ge(K.empty(("mod", m)), K.empty_count(("mod", m)))
        for q in range(4 * 4):
            ins = pe.transpose(K.bank(("mod", m))[:, 2 * q:2 * q + 2], K.hsT[0:2, 4 * m + q // 4, (q % 4) * P:(q % 4 + 1) * P],
                               ident[0:2, 0:2])
        ins.then_inc(K.full(("mod", m)), 1)
    for s in range(2):
        pe.wait_ge(K.sem["nrm"], K.count("nrm", 0, s + 1))
        for q in range(4):
            pe.wait_ge(K.empty(("hT", s, q)), K.empty_count(("hT", s, q)))
            bank = K.bank(("hT", s, q)).rearrange("p (k n) -> p k n", k=2)
            for j in range(2):
                for tt in range(TT):
                    ins = pe.transpose(bank[:, j, tt * P:(tt + 1) * P],
                                       K.nrm[:, s, tt, (2 * q + j) * P:(2 * q + j + 1) * P], ident)
            ins.then_inc(K.full(("hT", s, q)), 1)
    for s in range(2):
        for q in range(4):
            pe.wait_ge(K.empty(("hT", s, q)), K.drained_count(("hT", s, q)))

    pe.wait_ge(K.landed(("w2in", 7)), K.landed_count(("w2in", 7)))
    w = K.weights(("w2in", 7), DC, LAST_COLS)
    pe.wait_ge(K.sem["gate_w"], K.count("gate_w"))
    pe.wait_ge(K.empty(("lif", 0)), K.empty_count(("lif", 0)))
    product(K.bank(("lif", 0)), [(K.gate_w[:, kc, :], K.hsT[:, kc, :]) for kc in range(DC)], ("lif", 0))
    pe.wait_ge(K.empty(("lw", 0)), K.empty_count(("lw", 0)))
    bank = K.bank(("lw", 0))
    product(bank, [(w[:, kc, 32:160], K.hsT[:, kc, :]) for kc in range(DC)], ("lw", 0))
    pe.wait_ge(K.empty(("la", 0)), K.empty_count(("la", 0)))
    bank = K.bank(("la", 0))
    product(bank[0:64, :], [(w[:, kc, 160:224], K.hsT[:, kc, :]) for kc in range(DC)], ("la", 0))
    pe.wait_ge(K.empty(("lg", 0)), K.empty_count(("lg", 0)))
    bank = K.bank(("lg", 0))
    product(bank[:, 0:T], [(w[:, kc, 224:352], K.hsT[:, kc, T:]) for kc in range(DC)], ("lg", 0))

    def all_tokens(name, unit):
        pe.wait_ge(K.landed(("w2in", unit)), K.landed_count(("w2in", unit)))
        w = K.weights(("w2in", unit), DC, BANK)
        for c in range(4):
            pe.wait_ge(K.empty((name, c)), K.empty_count((name, c)))
            bank = K.bank((name, c))
            product(bank, [(w[:, kc, c * P:(c + 1) * P], K.hsT[:, kc, :]) for kc in range(DC)], (name, c))

    def latents(name, unit):
        pe.wait_ge(K.landed(("w2in", unit)), K.landed_count(("w2in", unit)))
        w = K.weights(("w2in", unit), DC, BANK)
        for i in range(2):
            pe.wait_ge(K.empty((name, i)), K.empty_count((name, i)))
            bank = K.bank((name, i))
            for j in range(2):
                c = 2 * i + j
                ins = product(bank[:, j * T:(j + 1) * T], [(w[:, kc, c * P:(c + 1) * P], K.hsT[:, kc, T:]) for kc in range(DC)])
            ins.then_inc(K.full((name, i)), 1)

    all_tokens("rk", 3)
    pe.wait_ge(K.sem["dma_lora"], K.count("dma_lora"))
    pe.wait_ge(K.empty(("la", 0)), K.drained_count(("la", 0)))
    for c in range(4):
        pe.wait_ge(K.empty(("al", c)), K.empty_count(("al", c)))
        bank = K.bank(("al", c))
        product(bank, [(K.aB[0:64, c * P:(c + 1) * P], K.laT[0:64, :])], ("al", c))
    pe.wait_ge(K.empty(("lw", 0)), K.drained_count(("lw", 0)))
    for z in range(ZS):
        for c in range(4):
            pe.wait_ge(K.empty(("wl", z, c)), K.empty_count(("wl", z, c)))
            bank = K.bank(("wl", z, c))
            product(bank, [(K.wB[64 * z:64 * z + 64, c * P:(c + 1) * P], K.lwT[64 * z:64 * z + 64, :])], ("wl", z, c))
    pe.wait_ge(K.empty(("lg", 0)), K.drained_count(("lg", 0)))
    for i in range(2):
        pe.wait_ge(K.empty(("gl", i)), K.empty_count(("gl", i)))
        bank = K.bank(("gl", i))
        for j in range(2):
            ins = product(bank[:, j * T:(j + 1) * T], [(K.gB[:, (2 * i + j) * P:(2 * i + j + 1) * P], K.lgT)])
        ins.then_inc(K.full(("gl", i)), 1)
    all_tokens("rv", 4)
    latents("rr", 2)
    all_tokens("mk", 1)
    for c in range(4):
        pe.wait_ge(K.sem["kap_sq"], K.count("kap_sq", 0, c + 1))
        pe.wait_ge(K.empty(("ss", c)), K.empty_count(("ss", c)))
        bank = K.bank(("ss", c))
        product(bank, [(K.head_ones, K.sq[:, c % 2, :])], ("ss", c))
    latents("mq", 0)
    pe.wait_ge(K.landed(("w2in", 5)), K.landed_count(("w2in", 5)))
    w = K.weights(("w2in", 5), DC, BANK)
    for i in range(SB):
        pe.wait_ge(K.empty(("mv", i)), K.empty_count(("mv", i)))
        bank = K.bank(("mv", i))
        product(bank, [(K.hsT[:, kc, i * P:(i + 1) * P], w[:, kc, :]) for kc in range(DC)], ("mv", i))
    latents("mo2", 6)
    for i in range(2):
        pe.wait_ge(K.sem["bonus_in"], K.count("bonus_in", 0, i + 1))
        pe.wait_ge(K.empty(("bs", i)), K.empty_count(("bs", i)))
        bank = K.bank(("bs", i))
        product(bank, [(K.head_ones, K.bonus_in[:, i, :])], ("bs", i))
    pe.wait_ge(K.sem["gates_ready"], K.count("gates_ready"))
    pe.wait_ge(K.empty(("gT", 0)), K.empty_count(("gT", 0)))
    bank = K.bank(("gT", 0))
    n = Z0 + HH
    for i in range(SB):
        ins = pe.transpose(bank[:, i * n:(i + 1) * n], K.g_row[0:n, i * P:(i + 1) * P], ident[0:n, 0:n])
    ins.then_inc(K.full(("gT", 0)), 1)

    for name in ("km", "qm", "pick"):
        pe.wait_ge(K.sem[name], K.count(name))
    for i in range(SB):
        pe.wait_ge(K.empty(("mv", i)), K.drained_count(("mv", i)))
    for h in range(HH):
        rows, c = slice((h % 2) * HD, (h % 2) * HD + HD), h // 2
        pe.wait_ge(K.empty(("bG", h)), K.empty_count(("bG", h)))
        bank = K.bank(("bG", h))
        for z in range(ZS):
            ins = product(bank[:, z * T:(z + 1) * T], [(K.pick[0:n, z, h, :], K.neg_G[0:n, :])])
        ins.then_inc(K.full(("bG", h)), 1)
        for i in range(2):
            pe.wait_ge(K.empty(("qk", h, i)), K.empty_count(("qk", h, i)))
            bank = K.bank(("qk", h, i))
            for j in range(2):
                s = 2 * i + j
                ins = product(bank[:, j * T:(j + 1) * T], [(K.km[rows, c, s * P:(s + 1) * P], K.qm[rows, c, :])])
            ins.then_inc(K.full(("qk", h, i)), 1)
        if h % 2 == 0:
            continue
        hp = h // 2
        pe.wait_ge(K.empty(("em", hp)), K.empty_count(("em", hp)))
        bank = K.bank(("em", hp))
        for hh in (h - 1, h):
            out = slice((hh % 2) * HD, (hh % 2) * HD + HD)
            for z in range(ZS):
                ins = product(bank[out, z * T:(z + 1) * T], [(K.pick[0:n, z, hh, 0:HD], K.neg_m[0:n, :])])
        ins.then_inc(K.full(("em", hp)), 1)
        pe.wait_ge(K.empty(("num", hp)), K.empty_count(("num", hp)))
        pe.wait_ge(K.empty(("den", hp)), K.empty_count(("den", hp)))
        num, den = K.bank(("num", hp)), K.bank(("den", hp))
        for hh in (h - 1, h):
            out = slice((hh % 2) * HD, (hh % 2) * HD + HD)
            for z in range(ZS):
                pe.wait_ge(K.sem["weights_m"], K.count("weights_m", 0, 2 * hh + z + 1))
                st = K.st[:, hh % 2, z, :, :]
                a = product(num[out, z * T:(z + 1) * T], [(K.mv[:, s, hh * HD:(hh + 1) * HD], st[:, s, :]) for s in range(SB)])
                ins = product(den[out, z * T:(z + 1) * T], [(K.ones[:, 0:HD], st[:, s, :]) for s in range(SB)])
        a.then_inc(K.full(("num", hp)), 1)
        ins.then_inc(K.full(("den", hp)), 1)
    head_norm_tensor(pe, K, "hm", "hv", "h_m", "hm_sq", K.mixed[:, 0:4, :])


def head_norm_tensor(pe, K, mean, var, ready, squared, src):
    for hp in range(HP):
        pe.wait_ge(K.sem[ready], K.count(ready, 0, hp + 1))
        pe.wait_ge(K.empty((mean, hp)), K.empty_count((mean, hp)))
        bank = K.bank((mean, hp))
        pe.matmul(bank[:, 0:T], K.head_mean, src[:, hp, :], start=True, stop=True).then_inc(K.full((mean, hp)), 1)
    for hp in range(HP):
        pe.wait_ge(K.sem[squared], K.count(squared, 0, hp + 1))
        pe.wait_ge(K.empty((var, hp)), K.empty_count((var, hp)))
        bank = K.bank((var, hp))
        pe.matmul(bank[:, 0:T], K.head_mean, K.hn_sq[:, hp % 2, :], start=True, stop=True).then_inc(K.full((var, hp)), 1)


def conv_taps():
    for dy in (-1, 0, 1):
        for dx in (-1, 0, 1):
            if (dy, dx) != (0, 0):
                yield dy, dx


def mid_scalar(act, K):
    link = Chain(K.act_done, K.act_base)

    def drain(key, dst, fn=ACT.Copy, n=BANK, parts=slice(None), src=lambda b: b, **kw):
        act.wait_ge(K.full(key), K.full_count(key))
        act.activation(dst, src(K.bank(key)[parts, 0:n]), fn, **kw).then_inc(K.empty(key), 1)

    act.wait_ge(K.empty(("bvec", 0)), K.drained_count(("bvec", 0)))
    col = lambda name, i=0, n=1: K.vec2[:, VROWS[name][0] + i:VROWS[name][0] + i + n]
    act.activation(K.c_col[:, :, 0], col("c", 0, DC), ACT.Silu)
    act.activation(K.c_col[:, :, 1], col("c_ctx", 0, DC), ACT.Silu).then_inc(K.sem["silu_c"], 1)
    for s in range(2):
        act.wait_ge(K.sem["nrm_var"], K.count("nrm_var", 0, s + 1))
        act.activation(K.nrm_std[:, s, :], K.nrm_mv[:, s, :, 1], ACT.Sqrt).then_inc(K.sem["nrm_std"], 1)
    for m in range(2):
        for i in range(4):
            drain(("mod_row", m, i), K.hsT[0:2, 4 * m + i, :], parts=slice(0, 2))
    act.wait_ge(K.sem["mod"], K.count("mod", 0, 1))
    for s in range(2):
        for q in range(4):
            act.wait_ge(K.full(("hT", s, q)), K.full_count(("hT", s, q)))
            bank = K.bank(("hT", s, q))
            for j in range(2):
                kc = 2 * q + j
                ins = act.activation(K.hsT[:, kc, s * T:(s + 1) * T], bank[:, j * T:(j + 1) * T], ACT.Identity,
                                     scale=K.mod[:, 0, DC + kc, 1 - s:2 - s], bias=K.mod[:, 0, kc, 1 - s:2 - s])
            ins.then_inc(K.empty(("hT", s, q)), 1)
    act.wait_ge(K.sem["gate_x"], K.count("gate_x"))
    for z in range(ZS):
        r = slice(Z0 * z, Z0 * z + HH)
        act.activation(K.row_t[r, :], K.lf_row[r, :], ACT.Abs).then_inc(link.sem, 1)
        act.wait_ge(link.sem, link.count())
        act.activation(K.row_t[r, :], K.row_t[r, :], ACT.Exp, scale=-1.0).then_inc(link.sem, 1)
        act.wait_ge(link.sem, link.count())
        ins = act.activation(K.row_t[r, :], K.row_t[r, :], ACT.Ln, bias=1.0)
    ins.then_inc(K.sem["gate_ln"], 1)
    drain(("lw", 0), K.lwT, ACT.Tanh)
    drain(("la", 0), K.laT[0:64, :], parts=slice(0, 64))
    drain(("lg", 0), K.lgT, ACT.Sigmoid, n=T)

    def centre(name, i, base, dst, n):
        act.wait_ge(K.full((name, i)), K.full_count((name, i)))
        bank = K.bank((name, i))
        if n == 1:
            act.activation(dst[:, i, :], bank, ACT.Copy, scale=K.taps[:, 4, base + i:base + i + 1]).then_inc(K.sem[name + "_center"], 1)
            return
        for j in range(2):
            c = 2 * i + j
            act.activation(dst[:, c, :], bank[:, j * T:(j + 1) * T], ACT.Copy,
                                    scale=K.taps[:, 4, base + c:base + c + 1]).then_inc(K.sem[name + "_center"], 1)

    for c in range(4):
        centre("rk", c, 12, K.kmod, 1)
    for c in range(4):
        drain(("al", c), K.aT[:, c, :], ACT.Sigmoid, bias=col("r_a0", c))
    for z in range(ZS):
        for c in range(4):
            if 4 * z + c >= 2:
                act.wait_ge(K.sem["cum"], K.count("cum", 0, 4 * z + c - 1))
            drain(("wl", z, c), K.sw[:, c % 2, :], ACT.Sigmoid, bias=col("r_w0", 4 * z + c))
    for i in range(2):
        drain(("gl", i), K.g_T[:, 2 * i:2 * i + 2, :], src=lambda b: b.rearrange("p (k n) -> p k n", k=2))
    for c in range(4):
        centre("rv", c, 16, K.rv, 1)
    for i in range(2):
        centre("rr", i, 8, K.r_T, 2)
    for c in range(4):
        centre("mk", c, 4, K.km, 1)
    for c in range(4):
        if c >= 2:
            act.wait_ge(K.sem["kh"], K.count("kh", 0, c - 1))
        act.wait_ge(K.full(("ss", c)), K.full_count(("ss", c)))
        act.activation(K.ss_root[:, c % 2, :], K.bank(("ss", c)), ACT.Sqrt).then_inc(K.sem["ss_root"], 1)
    for i in range(2):
        centre("mq", i, 0, K.qm, 2)
    for i in range(SB):
        drain(("mv", i), K.mv[:, i, :])
    for i in range(2):
        drain(("mo2", i), K.mixed_gate[:, 2 * i:2 * i + 2, :], ACT.Sigmoid, src=lambda b: b.rearrange("p (k n) -> p k n", k=2))
    act.wait_ge(K.sem["conv_mk"], K.count("conv_mk"))
    act.activation(K.km, K.km, ACT.Silu).then_inc(K.sem["km"], 1)
    act.wait_ge(K.sem["conv_mq"], K.count("conv_mq"))
    act.activation(K.qm, K.qm, ACT.Silu).then_inc(K.sem["qm"], 1)
    for h in range(HH):
        for z in range(ZS):
            n = 2 * h + z
            act.wait_ge(K.sem["expo_in"], K.count("expo_in", 0, n + 1))
            act.activation(K.st[:, h % 2, z, :, :], K.st[:, h % 2, z, :, :], ACT.Exp).then_inc(K.sem["expo"], 1)
        if h % 2:
            hp = h // 2
            if hp >= 1:
                act.wait_ge(K.sem["h_m"], K.count("h_m", 0, hp))
            drain(("em", hp), K.guard, ACT.Exp)
            drain(("den", hp), K.den_abs, ACT.Abs)
    head_norm_scalar(act, K, ("hv",), "hm_sq", "hm_var", "hm_std", "hm_c")


def head_norm_scalar(act, K, var, squared, v, std, centred):
    for hp in range(HP):
        act.wait_ge(K.sem[centred], K.count(centred, 0, hp + 1))
        if hp >= 2:
            act.wait_ge(K.full((var[0], hp - 2)), K.full_count((var[0], hp - 2)))
        act.activation(K.hn_sq[:, hp % 2, :], K.hn_c[:, hp, :], ACT.Square).then_inc(K.sem[squared], 1)
    for hp in range(HP):
        act.wait_ge(K.sem[v], K.count(v, 0, hp + 1))
        act.activation(K.hn_v[:, hp % 2, :], K.hn_v[:, hp % 2, :], ACT.Sqrt).then_inc(K.sem[std], 1)


def mid_gpsimd(pool, K):
    link = Chain(K.pool_done, K.pool_base)
    pool.wait_ge(K.sem["x_in"], K.count("x_in", DEPTH))
    pool.memset(K.vrows2, 0.0).then_inc(K.sem["rows_clear"], 1)
    for tile in (K.g_row, K.neg_G, K.neg_m, K.gate_w):
        pool.memset(tile, 0.0).then_inc(link.sem, 1)
        pool.wait_ge(link.sem, link.count())
    pool.memset(K.head_ones, 0.0).then_inc(link.sem, 1)
    pool.wait_ge(link.sem, link.count())
    for h in range(2):
        pool.memset(K.head_ones[h * HD:(h + 1) * HD, h * HD:(h + 1) * HD], 1.0).then_inc(link.sem, 1)
        pool.wait_ge(link.sem, link.count())
    pool.tensor_scalar(K.head_mean, K.head_ones, 1.0 / HD, None, ALU.mult).then_inc(link.sem, 1)
    pool.wait_ge(link.sem, link.count())
    pool.memset(K.go_on, 1.0).then_inc(link.sem, 1)
    pool.wait_ge(link.sem, link.count())
    for z in range(ZS):
        view = K.go_on[:, z, :].rearrange("p (c t) -> p c t", t=CH)
        at = 0 if z == 0 else CH - 1
        pool.memset(view[:, :, at:at + 1], 0.0).then_inc(link.sem, 1)
        pool.wait_ge(link.sem, link.count())
    pool.sem_inc(K.sem["zeros"], 1)
    pool.wait_ge(K.sem["cum"], K.count("cum"))
    for z in range(ZS):
        pool.tensor_copy(K.pick[:, z], K.ident[:, Z0 * z:Z0 * z + HH].unsqueeze(2).broadcast_to([P, HH, P])).then_inc(link.sem, 1)
        pool.wait_ge(link.sem, link.count())
    pool.sem_inc(K.sem["pick"], 1)
    for h in range(HH):
        for z in range(ZS):
            n = 2 * h + z
            pool.wait_ge(K.sem["expo"], K.count("expo", 0, n + 1))
            st = K.st[:, h % 2, z, SB // 2:, :]
            sign = 1 if z == 0 else -1
            pool.affine_select(out=st, in_=st, compare_op=ALU.is_ge, fill=0.0, base=0,
                                        pattern=[[-sign * P, SB // 2], [sign, T]], channel_multiplier=-sign).then_inc(K.sem["masked"], 1)
    K.pool_base = link.base + link.n


def mid_vector(dve, K):
    link = Chain(K.dve_done, K.dve_base)
    tt_op, ts_op, stt = dve.tensor_tensor, dve.tensor_scalar, dve.scalar_tensor_tensor
    col = lambda name, i=0, n=1: K.vec2[:, VROWS[name][0] + i:VROWS[name][0] + i + n]

    def stats(src, mv):
        for i in range(2):
            dve.bn_stats(K.bn2[:, i, :], src[:, i * BANK:(i + 1) * BANK]).then_inc(link.sem, 1)
            dve.wait_ge(link.sem, link.count())
        dve.bn_aggr(mv, K.bn2.rearrange("p a b -> p (a b)")).then_inc(link.sem, 1)
        dve.wait_ge(link.sem, link.count())

    dve.wait_ge(K.sem["zeros"], K.count("zeros"))
    dve.wait_ge(K.full(("bvec", 0)), K.full_count(("bvec", 0)))
    bank = K.bank(("bvec", 0))
    dve.tensor_copy(K.vec2, bank[:, 0:P])
    dve.tensor_copy(K.taps, bank[:, P:P + 9 * CONV_CHUNKS].rearrange("p (t c) -> p t c", c=CONV_CHUNKS)).then_inc(K.empty(("bvec", 0)), 1)
    for s in range(2):
        if s == 0:
            dve.wait_ge(K.sem["dma_ctx"], K.count("dma_ctx"))
        for tt in range(TT):
            stats(K.nrm[:, 0, tt, :] if s == 0 else K.x_tok[:, tt, :], K.nrm_mv[:, s, tt, :])
        ts_op(K.nrm_mv[:, s, :, 1], K.nrm_mv[:, s, :, 1], LN_EPS_2, None, ALU.add).then_inc(K.sem["nrm_var"], 1)
    for s in range(2):
        dve.wait_ge(K.sem["nrm_std"], K.count("nrm_std", 0, s + 1))
        dve.reciprocal(K.nrm_std[:, s, :], K.nrm_std[:, s, :]).then_inc(link.sem, 1)
        dve.wait_ge(link.sem, link.count())
        for tt in range(TT):
            src = K.nrm[:, 0, tt, :] if s == 0 else K.x_tok[:, tt, :]
            ins = ts_op(K.nrm[:, s, tt, :], src, K.nrm_mv[:, s, tt, 0:1], K.nrm_std[:, s, tt:tt + 1], ALU.subtract, ALU.mult)
        ins.then_inc(K.sem["nrm"], 1)
    dve.wait_ge(K.empty(("bvec", 0)), K.drained_count(("bvec", 0)))
    for m in range(2):
        dve.wait_ge(K.full(("mod", m)), K.full_count(("mod", m)))
        bank = K.bank(("mod", m))
        b = col("b_ada", 24 * m, 2 * DC).unsqueeze(2).broadcast_to([P, 2 * DC, 2])
        tt_op(K.mod[:, m], bank[:, 0:4 * DC].rearrange("p (k n) -> p k n", n=2), b, ALU.add).then_inc(K.empty(("mod", m)), 1)
        dve.wait_ge(K.empty(("mod", m)), K.drained_count(("mod", m)))
        ts_op(K.mod[:, m, DC:], K.mod[:, m, DC:], 1.0, None, ALU.add).then_inc(K.sem["mod"], 1)

    dve.wait_ge(K.landed(("w2in", 7)), K.landed_count(("w2in", 7)))
    w = K.weights(("w2in", 7), DC, LAST_COLS)
    for k, lo in enumerate((0, 16, 8, 24)):
        ins = dve.tensor_copy(K.gate_w[:, :, Z0 * k:Z0 * k + HH], w[:, :, lo:lo + HH])
    ins.then_inc(K.sem["gate_w"], 1)
    dve.wait_ge(K.full(("lif", 0)), K.full_count(("lif", 0)))
    bank = K.bank(("lif", 0))
    for z in range(ZS):
        r, f = slice(Z0 * z, Z0 * z + HH), slice(2 * Z0 + Z0 * z, 2 * Z0 + Z0 * z + HH)
        ts_op(K.li_row[r, :], bank[r, :], K.bias_i[r, :], None, ALU.add)
        ins = ts_op(K.lf_row[r, :], bank[f, :], K.bias_f[f, :], None, ALU.add)
    ins.then_inc(K.empty(("lif", 0)), 1)
    dve.wait_ge(K.empty(("lif", 0)), K.drained_count(("lif", 0)))
    dve.sem_inc(K.sem["gate_x"], 1)
    dve.wait_ge(K.sem["gate_ln"], K.count("gate_ln"))
    for z in range(ZS):
        r = slice(Z0 * z, Z0 * z + HH)
        stt(out=K.lf_row[r, :], in0=K.lf_row[r, :], scalar=0.0, in1=K.row_t[r, :], op0=ALU.min, op1=ALU.subtract).then_inc(link.sem, 1)
        dve.wait_ge(link.sem, link.count())
        dve.memset(K.row_t[r, :], 1.0).then_inc(link.sem, 1)
        dve.wait_ge(link.sem, link.count())
        b, g, G = K.b_row, K.g_row, K.G_row
        segs = [slice(0, S_ALL)] if z == 0 else [slice(T - 1, None, -1), slice(S_ALL - 1, T - 1, -1)]
        for i, seg in enumerate(segs):
            init = 0.0 if i == 0 else b[r, 0:1]
            dve.tensor_tensor_scan(b[r, seg], K.row_t[r, seg], K.lf_row[r, seg], init, ALU.mult, ALU.add).then_inc(link.sem, 1)
            dve.wait_ge(link.sem, link.count())
        tt_op(g[r, :], K.li_row[r, :], b[r, :], ALU.subtract).then_inc(link.sem, 1)
        dve.wait_ge(link.sem, link.count())
        for i, seg in enumerate(segs):
            init = 0.0 if i == 0 else G[r, 0:1]
            dve.tensor_tensor_scan(G[r, seg], g[r, seg], g[r, seg], init, ALU.max, ALU.max).then_inc(link.sem, 1)
            dve.wait_ge(link.sem, link.count())
        ts_op(K.neg_G[r, :], G[r, T:], -1.0, None, ALU.mult).then_inc(link.sem, 1)
        dve.wait_ge(link.sem, link.count())
        ins = tt_op(K.neg_m[r, :], K.neg_G[r, :], b[r, T:], ALU.subtract)
        if z == 1:
            ins.then_inc(K.sem["gates_ready"], 1)
        else:
            ins.then_inc(link.sem, 1)
            dve.wait_ge(link.sem, link.count())

    def conv(name, key, dst, c, base, lat_only):
        dve.wait_ge(K.full(key), K.full_count(key))
        bank = K.bank(key)
        dve.wait_ge(K.sem[name + "_center"], K.count(name + "_center", 0, 2 * (c // 2) + 2 if lat_only else c + 1))
        lat_in = bank[:, T:] if not lat_only else bank[:, (c % 2) * T:(c % 2 + 1) * T]
        lat_out = dst[:, c, T:] if not lat_only else dst[:, c, :]
        grid = lambda a: a.rearrange("p (y x) -> p y x", x=64)
        last = None
        for dy, dx in conv_taps():
            w = K.taps[:, 3 * (dy + 1) + dx + 1, base + c:base + c + 1]
            for ctx in ((False,) if lat_only or dy else (False, True)):
                if last is not None:
                    last.then_inc(link.sem, 1)
                    dve.wait_ge(link.sem, link.count())
                if ctx:
                    o, i = dst[:, c, max(0, -dx):T - max(0, dx)], bank[:, max(0, dx):T - max(0, -dx)]
                else:
                    ys, xs = slice(max(0, -dy), 4 - max(0, dy)), slice(max(0, -dx), 64 - max(0, dx))
                    yi, xi = slice(max(0, dy), 4 - max(0, -dy)), slice(max(0, dx), 64 - max(0, -dx))
                    o, i = grid(lat_out)[:, ys, xs], grid(lat_in)[:, yi, xi]
                last = stt(out=o, in0=i, scalar=w, in1=o, op0=ALU.mult, op1=ALU.add)
        return last

    for c in range(4):
        conv("rk", ("rk", c), K.kmod, c, 12, False).then_inc(K.empty(("rk", c)), 1)
        dve.wait_ge(K.empty(("rk", c)), K.drained_count(("rk", c)))
    for z in range(ZS):
        for c in range(4):
            dve.wait_ge(K.empty(("wl", z, c)), K.drained_count(("wl", z, c)))
            step = slice(None) if z == 0 else slice(None, None, -1)
            dve.tensor_tensor_scan(K.cum[:, z, c, step], K.go_on[:, z, step], K.sw[:, c % 2, step], 0.0,
                                            ALU.mult, ALU.add).then_inc(K.sem["cum"], 1)
    for c in range(4):
        ts_op(K.kh[:, c, :], K.kmod[:, c, :], col("r_kk", c), None, ALU.mult).then_inc(link.sem, 1)
        dve.wait_ge(link.sem, link.count())
    for c in range(2):
        tt_op(K.sq[:, c % 2, :], K.kh[:, c, :], K.kh[:, c, :], ALU.mult).then_inc(K.sem["kap_sq"], 1)
    for c in range(4):
        dve.wait_ge(K.empty(("al", c)), K.drained_count(("al", c)))
        ts_op(K.tmp2[:, 0, :], K.aT[:, c, :], -1.0, col("r_ka", c), ALU.add, ALU.mult).then_inc(link.sem, 1)
        dve.wait_ge(link.sem, link.count())
        stt(out=K.kmod[:, c, :], in0=K.tmp2[:, 0, :], scalar=1.0, in1=K.kmod[:, c, :], op0=ALU.add, op1=ALU.mult).then_inc(link.sem, 1)
        dve.wait_ge(link.sem, link.count())
    for c in range(4):
        conv("rv", ("rv", c), K.rv, c, 16, False).then_inc(K.empty(("rv", c)), 1)
        dve.wait_ge(K.empty(("rv", c)), K.drained_count(("rv", c)))
    for c in range(4):
        last = conv("rr", ("rr", c // 2), K.r_T, c, 8, True)
        if c % 2 == 0:
            last.then_inc(link.sem, 1)
            dve.wait_ge(link.sem, link.count())
        else:
            last.then_inc(K.empty(("rr", c // 2)), 1)
    dve.wait_ge(K.empty(("rr", 1)), K.drained_count(("rr", 1)))
    for i in range(2):
        for j in range(2):
            c = 2 * i + j
            ins = stt(out=K.bonus_in[:, i, j * T:(j + 1) * T], in0=K.r_T[:, c, :], scalar=col("r_bonus", c),
                      in1=K.kmod[:, c, T:], op0=ALU.mult, op1=ALU.mult)
        ins.then_inc(K.sem["bonus_in"], 1)
    for c in range(4):
        last = conv("mk", ("mk", c), K.km, c, 4, False)
        last.then_inc(K.empty(("mk", c)), 1)
        dve.wait_ge(K.empty(("mk", c)), K.drained_count(("mk", c)))
    dve.sem_inc(K.sem["conv_mk"], 4)
    for c in range(4):
        dve.wait_ge(K.sem["ss_root"], K.count("ss_root", 0, c + 1))
        root = K.ss_root[:, c % 2, :]
        ts_op(root, root, 1e-12, None, ALU.max).then_inc(link.sem, 1)
        dve.wait_ge(link.sem, link.count())
        dve.reciprocal(root, root).then_inc(link.sem, 1)
        dve.wait_ge(link.sem, link.count())
        tt_op(K.kh[:, c, :], K.kh[:, c, :], root, ALU.mult).then_inc(K.empty(("ss", c)), 1)
        dve.wait_ge(K.empty(("ss", c)), K.drained_count(("ss", c)))
        tt_op(K.aT[:, c, :], K.aT[:, c, :], K.kh[:, c, :], ALU.mult).then_inc(K.sem["kh"], 1)
        if c < 2:
            tt_op(K.sq[:, c % 2, :], K.kh[:, c + 2, :], K.kh[:, c + 2, :], ALU.mult).then_inc(K.sem["kap_sq"], 1)
    for c in range(4):
        last = conv("mq", ("mq", c // 2), K.qm, c, 0, True)
        if c % 2 == 0:
            last.then_inc(link.sem, 1)
            dve.wait_ge(link.sem, link.count())
        else:
            last.then_inc(K.empty(("mq", c // 2)), 1)
    dve.wait_ge(K.empty(("mq", 1)), K.drained_count(("mq", 1)))
    dve.sem_inc(K.sem["conv_mq"], 4)
    for i in range(2):
        dve.wait_ge(K.full(("bs", i)), K.full_count(("bs", i)))
        bank = K.bank(("bs", i)).rearrange("p (k n) -> p k n", k=2)
        tt_op(K.bonus[:, 2 * i:2 * i + 2, :], bank, K.rv[:, 2 * i:2 * i + 2, T:], ALU.mult).then_inc(K.empty(("bs", i)), 1)
    n = Z0 + HH
    dve.wait_ge(K.full(("gT", 0)), K.full_count(("gT", 0)))
    dve.tensor_copy(K.g_col, K.bank(("gT", 0))[:, 0:SB * n].rearrange("p (s r) -> p s r", r=n)).then_inc(K.empty(("gT", 0)), 1)
    dve.wait_ge(K.empty(("gT", 0)), K.drained_count(("gT", 0)))

    for h in range(HH):
        dve.wait_ge(K.full(("bG", h)), K.full_count(("bG", h)))
        bank = K.bank(("bG", h))
        if h >= 2:
            dve.wait_ge(K.full(("den", (h - 2) // 2)), K.full_count(("den", (h - 2) // 2)))
        for z in range(ZS):
            for s in range(SB):
                ins = ts_op(K.st[:, h % 2, z, s, :], bank[:, z * T:(z + 1) * T],
                            K.g_col[:, s, Z0 * z + h:Z0 * z + h + 1], 0.0, ALU.add, ALU.min)
            if z == 0:
                ins.then_inc(K.sem["expo_in"], 1)
        ins.then_inc(K.empty(("bG", h)), 1)
        dve.wait_ge(K.empty(("bG", h)), K.drained_count(("bG", h)))
        dve.sem_inc(K.sem["expo_in"], 1)
        for z in range(ZS):
            dve.wait_ge(K.sem["masked"], K.count("masked", 0, 2 * h + z + 1))
            for i in range(2):
                dve.wait_ge(K.full(("qk", h, i)), K.full_count(("qk", h, i)))
                bank = K.bank(("qk", h, i)).rearrange("p (k n) -> p k n", k=2)
                part = K.st[:, h % 2, z, 2 * i:2 * i + 2, :]
                ins = stt(out=part, in0=part, scalar=HD ** -0.5, in1=bank, op0=ALU.mult, op1=ALU.mult)
                if z == 1:
                    ins.then_inc(K.empty(("qk", h, i)), 1)
            if z == 1:
                dve.wait_ge(K.empty(("qk", h, 0)), K.drained_count(("qk", h, 0)))
                dve.wait_ge(K.empty(("qk", h, 1)), K.drained_count(("qk", h, 1)))
                dve.sem_inc(K.sem["weights_m"], 1)
            else:
                ins.then_inc(K.sem["weights_m"], 1)
        if h % 2:
            hp = h // 2
            dve.wait_ge(K.empty(("em", hp)), K.drained_count(("em", hp)))
            dve.wait_ge(K.empty(("den", hp)), K.drained_count(("den", hp)))
            tt_op(K.den_abs, K.den_abs, K.guard, ALU.max).then_inc(link.sem, 1)
            dve.wait_ge(link.sem, link.count())
            dve.reciprocal(K.den_abs, K.den_abs).then_inc(link.sem, 1)
            dve.wait_ge(link.sem, link.count())
            dve.wait_ge(K.full(("num", hp)), K.full_count(("num", hp)))
            tt_op(K.guard, K.den_abs, K.bank(("num", hp)), ALU.mult).then_inc(K.empty(("num", hp)), 1)
            dve.wait_ge(K.empty(("num", hp)), K.drained_count(("num", hp)))
            tt_op(K.mixed[:, hp, :], K.guard[:, 0:T], K.guard[:, T:], ALU.add).then_inc(K.sem["h_m"], 1)
            dve.wait_ge(K.sem["h_m"], K.count("h_m", 0, hp + 1))
    head_norm_vector(dve, K, link, "hm", "hv", "hm_c", "hm_var", "hm_std", K.mixed[:, 0:4, :], LN_EPS_2)
    for hp in range(HP):
        ts_op(K.mixed[:, hp, :], K.hn_c[:, hp, :], col("m_norm_w", hp), None, ALU.mult).then_inc(link.sem, 1)
        dve.wait_ge(link.sem, link.count())
        ins = tt_op(K.mixed[:, hp, :], K.mixed[:, hp, :], K.mixed_gate[:, hp, :], ALU.mult)
        if hp < HP - 1:
            ins.then_inc(link.sem, 1)
            dve.wait_ge(link.sem, link.count())
        else:
            ins.then_inc(K.sem["h_m_done"], 1)
    dve.wait_ge(K.sem["h_m_done"], K.count("h_m_done"))
    t = K.step[1]
    for tile, value in ((t.kr, 0.0), (t.b, 0.0), (t.k, 0.0), (t.v, 0.0), (t.s, 0.0), (t.p, 1.0)):
        ins = dve.memset(tile, value)
    ins.then_inc(K.sem["chunk_zeros"], 1)
    K.dve_base = link.base + link.n


def head_norm_vector(dve, K, link, mean, var, centred, v, std, src, eps):
    for hp in range(HP):
        dve.wait_ge(K.full((mean, hp)), K.full_count((mean, hp)))
        dve.tensor_tensor(K.hn_c[:, hp, :], src[:, hp, :], K.bank((mean, hp))[:, 0:T], ALU.subtract).then_inc(K.empty((mean, hp)), 1)
        dve.wait_ge(K.empty((mean, hp)), K.drained_count((mean, hp)))
        dve.sem_inc(K.sem[centred], 1)
    for hp in range(HP):
        if hp >= 2:
            norm(dve, K, link, hp - 2, std)
        dve.wait_ge(K.full((var, hp)), K.full_count((var, hp)))
        dve.tensor_scalar(K.hn_v[:, hp % 2, :], K.bank((var, hp))[:, 0:T], eps, None, ALU.add).then_inc(K.empty((var, hp)), 1)
        dve.wait_ge(K.empty((var, hp)), K.drained_count((var, hp)))
        dve.sem_inc(K.sem[v], 1)
    for hp in range(HP - 2, HP):
        norm(dve, K, link, hp, std)


def norm(dve, K, link, hp, std):
    dve.wait_ge(K.sem[std], K.count(std, 0, hp + 1))
    dve.reciprocal(K.hn_v[:, hp % 2, :], K.hn_v[:, hp % 2, :]).then_inc(link.sem, 1)
    dve.wait_ge(link.sem, link.count())
    dve.tensor_tensor(K.hn_c[:, hp, :], K.hn_c[:, hp, :], K.hn_v[:, hp % 2, :], ALU.mult).then_inc(link.sem, 1)
    dve.wait_ge(link.sem, link.count())


def chunk_at(i, z, first):
    return i * CH + first if z == 0 else i * -CH + (first + T - CH)


def chunk_start(eng, K, lat):
    eng.wait_ge(K.sem["chunk_zeros"], K.count("chunk_zeros"))
    if lat:
        for z in range(ZS):
            eng.wait_ge(K.empty(("ctx", "s", z)), K.drained_count(("ctx", "s", z), T // CH - 1))


def chunk_tensor(pe, K, ph, lat):
    ident = K.ident
    chunk_start(pe, K, lat)
    with pe.Fori(0, T // CH) as i:
        def product(out, *pairs_):
            for n, (a, b) in enumerate(pairs_):
                ins = pe.matmul(out, a, b, start=n == 0, stop=n == len(pairs_) - 1)
            return ins

        def four(name, z, fn, n=P):
            key = (ph, *name, z)
            pe.wait_ge(K.empty(key), K.empty_count(key, i))
            bank = K.bank(key)
            for u in range(HP):
                ins = product(bank[:, u * n:(u + 1) * n], *fn(u))
            ins.then_inc(K.full(key), 1)

        n = P + CH if lat else P
        for z in range(ZS):
            t = K.step[z]
            pe.wait_ge(K.sem[f"{ph}_hats"], K.count(f"{ph}_hats", i, z + 1))
            for name, w in (("mT", t.b), ("nT", t.k)):
                for j in range(2):
                    pe.wait_ge(K.empty((ph, name, z, j)), K.empty_count((ph, name, z, j), i))
                    bank = K.bank((ph, name, z, j))
                    for u in (2 * j, 2 * j + 1):
                        ins = product(bank[:, (u % 2) * n:(u % 2 + 1) * n], (w[:, u, :], t.kr[:, u, 0:n]))
                    ins.then_inc(K.full((ph, name, z, j)), 1)
            four(("m",), z, lambda u: [(t.kr[:, u, 0:P], t.b[:, u, :])])
            pe.wait_ge(K.sem[f"{ph}_v_blocks"], K.count(f"{ph}_v_blocks", i, z + 1))
            for name, src in (("bt", t.b), ("kt", t.k), ("vt", t.v)):
                pe.wait_ge(K.empty((ph, name, z)), K.empty_count((ph, name, z), i))
                bank = K.bank((ph, name, z))
                for u in range(HP):
                    ins = pe.transpose(bank[:, u * P:(u + 1) * P], src[:, u, :], ident)
                ins.then_inc(K.full((ph, name, z)), 1)
        for lv in range(1, LEVELS + 1):
            for z in range(ZS):
                t = K.step[z]
                if lv == 1:
                    pe.wait_ge(K.sem[f"{ph}_inv_start"], K.count(f"{ph}_inv_start", i, z + 1))
                    pe.wait_ge(K.empty((ph, "m", z)), K.drained_count((ph, "m", z), i))
                else:
                    if lv < LEVELS:
                        pe.wait_ge(K.empty((ph, "pow", lv - 1, z)), K.drained_count((ph, "pow", lv - 1, z), i))
                    pe.wait_ge(K.empty((ph, "powT", lv - 1, z)), K.drained_count((ph, "powT", lv - 1, z), i))
                    if lv > 2:
                        pe.wait_ge(K.empty((ph, "inv", lv - 1, z)), K.drained_count((ph, "inv", lv - 1, z), i))
                    four(("inv", lv), z, lambda u: [(t.zt[:, u, :], t.inv[:, u, :])])
                if lv < LEVELS - 1:
                    four(("pow", lv), z, lambda u: [(t.zt[:, u, :], t.z[:, u, :])])
                if lv < LEVELS:
                    four(("powT", lv), z, lambda u: [(t.z[:, u, :], t.zt[:, u, :])])
        for z in range(ZS):
            t = K.step[z]
            pe.wait_ge(K.empty((ph, "nT", z, 1)), K.drained_count((ph, "nT", z, 1), i))
            pe.wait_ge(K.empty((ph, "vt", z)), K.drained_count((ph, "vt", z), i))
            pe.wait_ge(K.empty((ph, "s", z)), K.drained_count((ph, "s", z), i, ago=1))
            four(("a1",), z, lambda u: [(t.kr[:, u, 0:P], t.s[:, u, :]), (t.nt[:, u, :], t.vt[:, u, :])])
        for z in range(ZS):
            t = K.step[z]
            pe.wait_ge(K.empty((ph, "inv", LEVELS, z)), K.drained_count((ph, "inv", LEVELS, z), i))
            pe.wait_ge(K.empty((ph, "a1", z)), K.drained_count((ph, "a1", z), i))
            four(("u",), z, lambda u: [(t.inv[:, u, :], t.a1[:, u, :])])
        if lat:
            for z in range(ZS):
                t = K.step[z]
                pe.wait_ge(K.empty((ph, "u", z)), K.drained_count((ph, "u", z), i))
                four(("y",), z, lambda u: [(t.s[:, u, :], t.kr[:, u, P:]), (t.u[:, u, :], t.rb[:, u, :]), (t.vt[:, u, :], t.rk[:, u, :])], CH)
        for z in range(ZS):
            t = K.step[z]
            pe.wait_ge(K.empty((ph, "u", z)), K.drained_count((ph, "u", z), i))
            pe.wait_ge(K.empty((ph, "bt", z)), K.drained_count((ph, "bt", z), i))
            pe.wait_ge(K.empty((ph, "kt", z)), K.drained_count((ph, "kt", z), i))
            four(("s",), z, lambda u: [(t.bt[:, u, :], t.u[:, u, :]), (t.kt[:, u, :], t.vt[:, u, :])])


def by_pair(bank, n=P):
    return bank[:, 0:HP * n].rearrange("p (u n) -> p u n", u=HP)


def chunk_scalar(act, K, ph, lat):
    first = T if lat else 0
    chunk_start(act, K, lat)
    with act.Fori(0, T // CH) as i:
        for z in range(ZS):
            t = K.step[z]
            act.wait_ge(K.empty((ph, "s", z)), K.drained_count((ph, "s", z), i, ago=1))
            cum = K.cum[:, z, :, bass.ds(chunk_at(i, z, first), CH)]
            at = 1 if z == 0 else 0
            act.activation(t.p[:, :, at:at + CH], cum, ACT.Exp, scale=-DECAY_SCALE)
            act.activation(t.p_inv, cum, ACT.Exp, scale=DECAY_SCALE).then_inc(K.sem[f"{ph}_decay"], 1)

        def copy(name, z, dst, **kw):
            key = (ph, *name, z)
            act.wait_ge(K.full(key), K.full_count(key, i))
            act.activation(dst, by_pair(K.bank(key)), ACT.Copy, **kw).then_inc(K.empty(key), 1)

        for z in range(ZS):
            t = K.step[z]
            copy(("bt",), z, t.bt, scale=-1.0)
            copy(("kt",), z, t.kt)
            copy(("vt",), z, t.vt)
        for lv in range(1, LEVELS):
            for z in range(ZS):
                t = K.step[z]
                act.wait_ge(K.full((ph, "powT", lv, z)), K.full_count((ph, "powT", lv, z), i))
                if lv < LEVELS - 1:
                    copy(("pow", lv), z, t.z)
                copy(("powT", lv), z, t.zt)
        for name in ("a1", "u"):
            for z in range(ZS):
                copy((name,), z, K.step[z].a1 if name == "a1" else K.step[z].u)


def chunk_gpsimd(pool, K, ph, lat):
    first = T if lat else 0
    chunk_start(pool, K, lat)
    with pool.Fori(0, T // CH) as i:
        for z in range(ZS):
            t = K.step[z]
            pool.wait_ge(K.empty((ph, "s", z)), K.drained_count((ph, "s", z), i, ago=1))
            for h in range(2):
                r = slice(h * HD, (h + 1) * HD)
                ins = pool.tensor_copy(t.v[r, :, h * CH:(h + 1) * CH], K.rv[r, :, bass.ds(chunk_at(i, z, first), CH)])
            ins.then_inc(K.sem[f"{ph}_v_blocks"], 1)


def chunk_vector(dve, K, ph, lat):
    first = T if lat else 0
    tt_op, stt = dve.tensor_tensor, dve.scalar_tensor_tensor
    chunk_start(dve, K, lat)
    with dve.Fori(0, T // CH) as i:
        for z in range(ZS):
            t = K.step[z]
            before, upto = (t.p[:, :, 0:CH], t.p[:, :, 1:CH + 1]) if z == 0 else (t.p[:, :, 1:CH + 1], t.p[:, :, 0:CH])
            at = bass.ds(chunk_at(i, z, first), CH)
            dve.wait_ge(K.empty((ph, "s", z)), K.drained_count((ph, "s", z), i, ago=1))
            dve.wait_ge(K.sem[f"{ph}_decay"], K.count(f"{ph}_decay", i, z + 1))
            for h in range(2):
                r, d = slice(h * HD, (h + 1) * HD), slice(h * CH, (h + 1) * CH)
                tt_op(t.kr[r, :, d], K.kh[r, :, at], before[r], ALU.mult)
                tt_op(t.b[r, :, d], K.aT[r, :, at], t.p_inv[r], ALU.mult)
                ins = tt_op(t.k[r, :, d], K.kmod[r, :, at], t.p_inv[r], ALU.mult)
            if lat:
                ins = tt_op(t.kr[:, :, P:], K.r_T[:, :, bass.ds(chunk_at(i, z, 0), CH)], upto, ALU.mult)
            ins.then_inc(K.sem[f"{ph}_hats"], 1)
        n = P + CH if lat else P
        halves = lambda bank: bank[:, 0:2 * n].rearrange("p (u n) -> p u n", u=2)
        for z in range(ZS):
            t = K.step[z]
            strict, turned = K.neg_mask[:, z, :], K.neg_mask[:, 1 - z, :]
            upto = K.upto_mask[:, z, :].unsqueeze(1).broadcast_to([P, 2, CH])
            for j in range(2):
                u = slice(2 * j, 2 * j + 2)
                mask = strict.unsqueeze(1).broadcast_to([P, 2, P])
                dve.wait_ge(K.full((ph, "mT", z, j)), K.full_count((ph, "mT", z, j), i))
                bank = halves(K.bank((ph, "mT", z, j)))
                ins = tt_op(t.z[:, u, :], bank[:, :, 0:P], mask, ALU.mult)
                if lat:
                    ins = stt(out=t.rb[:, u, :], in0=bank[:, :, P:], scalar=-1.0, in1=upto, op0=ALU.mult, op1=ALU.mult)
                ins.then_inc(K.empty((ph, "mT", z, j)), 1)
            key = (ph, "m", z)
            dve.wait_ge(K.full(key), K.full_count(key, i))
            tt_op(t.zt, by_pair(K.bank(key)), turned.unsqueeze(1).broadcast_to([P, HP, P]), ALU.mult).then_inc(K.empty(key), 1)
            dve.wait_ge(K.empty((ph, "mT", z, 1)), K.drained_count((ph, "mT", z, 1), i))
            dve.wait_ge(K.empty((ph, "mT", z, 0)), K.drained_count((ph, "mT", z, 0), i))
            tt_op(t.inv, t.z, K.ident.unsqueeze(1).broadcast_to([P, HP, P]), ALU.add).then_inc(K.sem[f"{ph}_inv_start"], 1)
            for j in range(2):
                u = slice(2 * j, 2 * j + 2)
                mask = strict.unsqueeze(1).broadcast_to([P, 2, P])
                dve.wait_ge(K.full((ph, "nT", z, j)), K.full_count((ph, "nT", z, j), i))
                bank = halves(K.bank((ph, "nT", z, j)))
                ins = stt(out=t.nt[:, u, :], in0=bank[:, :, 0:P], scalar=-1.0, in1=mask, op0=ALU.mult, op1=ALU.mult)
                if lat:
                    ins = tt_op(t.rk[:, u, :], bank[:, :, P:], upto, ALU.mult)
                ins.then_inc(K.empty((ph, "nT", z, j)), 1)
        for lv in range(2, LEVELS + 1):
            for z in range(ZS):
                t, key = K.step[z], (ph, "inv", lv, z)
                if lv == 2:
                    dve.wait_ge(K.sem[f"{ph}_inv_start"], K.count(f"{ph}_inv_start", i, z + 1))
                else:
                    dve.wait_ge(K.empty((ph, "inv", lv - 1, z)), K.drained_count((ph, "inv", lv - 1, z), i))
                dve.wait_ge(K.full(key), K.full_count(key, i))
                tt_op(t.inv, t.inv, by_pair(K.bank(key)), ALU.add).then_inc(K.empty(key), 1)
        if lat:
            for z in range(ZS):
                key, at = (ph, "y", z), bass.ds(chunk_at(i, z, 0), CH)
                if z == 1:
                    dve.wait_ge(K.empty((ph, "y", 0)), K.drained_count((ph, "y", 0), i))
                else:
                    dve.wait_ge(K.empty((ph, "y", 1)), K.drained_count((ph, "y", 1), i, ago=1))
                dve.wait_ge(K.full(key), K.full_count(key, i))
                tt_op(K.y_sum[:, :, at], K.y_sum[:, :, at], by_pair(K.bank(key), CH), ALU.add).then_inc(K.empty(key), 1)
        for z in range(ZS):
            t, key = K.step[z], (ph, "s", z)
            last = t.p[:, :, CH:CH + 1] if z == 0 else t.p[:, :, 0:1]
            dve.wait_ge(K.full(key), K.full_count(key, i))
            tt_op(t.s, t.s, by_pair(K.bank(key)), ALU.add).then_inc(K.sem[f"{ph}_sum"], 1)
            dve.wait_ge(K.sem[f"{ph}_sum"], K.count(f"{ph}_sum", i, z + 1))
            tt_op(t.s, t.s, last.broadcast_to([P, HP, P]), ALU.mult).then_inc(K.empty(key), 1)


def chunk_tiles_gpsimd(pool, K):
    link = Chain(K.pool_done, K.pool_base)
    pool.memset(K.earlier, 1.0).then_inc(link.sem, 1)
    pool.wait_ge(link.sem, link.count())
    pool.affine_select(out=K.earlier, in_=K.earlier, compare_op=ALU.is_gt, fill=0.0, base=0, pattern=[[1, P]],
                       channel_multiplier=-1).then_inc(link.sem, 1)
    pool.wait_ge(link.sem, link.count())
    for z in range(ZS):
        m = K.neg_mask[:, z, :]
        sign = 1 if z == 0 else -1
        pool.tensor_scalar(m, K.head_ones, -1.0, None, ALU.mult).then_inc(link.sem, 1)
        pool.wait_ge(link.sem, link.count())
        pool.affine_select(out=m, in_=m, compare_op=ALU.is_gt, fill=0.0, base=0, pattern=[[sign, P]], channel_multiplier=-sign).then_inc(link.sem, 1)
        pool.wait_ge(link.sem, link.count())
        for h in range(2):
            m = K.upto_mask[h * HD:(h + 1) * HD, z, :]
            pool.memset(m, 1.0).then_inc(link.sem, 1)
            pool.wait_ge(link.sem, link.count())
            pool.affine_select(out=m, in_=m, compare_op=ALU.is_ge, fill=0.0, base=0, pattern=[[sign, CH]], channel_multiplier=-sign).then_inc(link.sem, 1)
            pool.wait_ge(link.sem, link.count())
    pool.iota(K.rank, pattern=[[-1, EXPERTS]], base=EXPERTS, channel_multiplier=0, allow_small_or_imprecise_dtypes=True).then_inc(link.sem, 1)
    pool.wait_ge(link.sem, link.count())
    pool.wait_ge(K.sem["h_m_done"], K.count("h_m_done"))
    t = K.step[0]
    for tile, value in ((t.kr, 0.0), (t.b, 0.0), (t.k, 0.0), (t.v, 0.0), (t.s, 0.0), (t.p, 1.0)):
        pool.memset(tile, value).then_inc(link.sem, 1)
        pool.wait_ge(link.sem, link.count())
    pool.memset(K.y_sum, 0.0).then_inc(link.sem, 1)
    pool.wait_ge(link.sem, link.count())
    K.pool_base = link.base + link.n
    pool.sem_inc(K.sem["chunk_zeros"], 1)


def tail_sync(sp, K, A):
    rows = lambda a: a[0].rearrange("(k p) n -> p k n", p=P)
    for kind, c in tail_units():
        if (kind, c) == ("wo2", 0):
            sp.wait_ge(K.sem["c_rows"], K.count("c_rows"))
            def put(dst, src):
                sp.dma_start(dst, src).then_inc(K.sem["dma_tail"], 16)
            for i, a in enumerate((A["ln1_g_2"], A["ln1_b_2"], A["ln2_g_2"], A["ln2_b_2"])):
                put(K.ln2_rows[:, i, :], a.broadcast_to([P, D]))
            for i, part in enumerate((2, 5)):
                put(K.g_bias[:, i, :], A["b_ada_2"][0:1, part * D:(part + 1) * D].broadcast_to([P, D]))
            put(K.rt_w[:, :, 0:GROUPS_E], rows(A["rt_g_2"]))
            put(K.rt_w[:, :, GROUPS_E:], rows(A["rt_e_2"]))
            put(K.rt_bias[0:1, GROUPS_E:], A["rt_e_b_2"])
        src = A["w_ada_2"] if kind == "ada" else A["w_out_2"]
        sp.wait_ge(K.used_up((kind, c)), K.free_count((kind, c)))
        weights = rows(src)[:, :, c * BANK:(c + 1) * BANK]
        sp.dma_start(K.slot_like((kind, c), weights), weights).then_inc(K.landed((kind, c)), 16)


def tail_tensor(pe, K):
    def gate_rows(name, units):
        for i, u in enumerate(units):
            pe.wait_ge(K.landed(("ada", u)), K.landed_count(("ada", u)))
            w = K.weights(("ada", u), DC, BANK)
            pe.wait_ge(K.empty((name, i)), K.empty_count((name, i)))
            bank = K.bank((name, i))
            for kc in range(DC):
                ins = pe.matmul(bank, K.c_rows[:, kc, :], w[:, kc, :], start=kc == 0, stop=kc == DC - 1)
            ins.then_inc(K.full((name, i)), 1)

    head_norm_tensor(pe, K, "ym", "yv", "y_ready", "y_sq", K.y_sum)
    pe.wait_ge(K.sem["c_rows"], K.count("c_rows"))
    gate_rows("g1", (4, 5))
    pe.wait_ge(K.sem["mixed_r"], K.count("mixed_r"))
    for hf in range(2):
        pe.wait_ge(K.landed(("wo2", hf)), K.landed_count(("wo2", hf)))
        w = K.weights(("wo2", hf), DC, BANK)
        for tt in range(TT):
            pe.wait_ge(K.empty(("out2", tt, hf)), K.empty_count(("out2", tt, hf)))
            bank = K.bank(("out2", tt, hf))
            for kc in range(DC):
                ins = pe.matmul(bank, K.mixed[:, kc, tt * P:(tt + 1) * P], w[:, kc, :], start=kc == 0, stop=kc == DC - 1)
            ins.then_inc(K.full(("out2", tt, hf)), 1)
    for q in range(4):
        pe.wait_ge(K.empty(("h2T", q)), K.empty_count(("h2T", q)))
        bank = K.bank(("h2T", q)).rearrange("p (k n) -> p k n", k=2)
        for j in range(2):
            for tt in range(TT):
                pe.wait_ge(K.sem["x4"], K.count("x4", 0, tt + 1))
                ins = pe.transpose(bank[:, j, tt * P:(tt + 1) * P], K.x_hat[:, tt, (2 * q + j) * P:(2 * q + j + 1) * P], K.ident)
        ins.then_inc(K.full(("h2T", q)), 1)
    for q in range(4):
        pe.wait_ge(K.empty(("h2T", q)), K.drained_count(("h2T", q)))
    pe.wait_ge(K.sem["dma_tail"], K.count("dma_tail"))
    for tt in range(TT):
        pe.wait_ge(K.empty(("rt", tt)), K.empty_count(("rt", tt)))
        bank = K.bank(("rt", tt))
        out = bank[:, 0:GROUPS_E + EXPERTS]
        for kc in range(DC):
            pe.matmul(out, K.h2T[:, kc, tt * P:(tt + 1) * P], K.rt_w[:, kc, :], start=kc == 0, stop=False)
        pe.matmul(out, K.ones[0:1, :], K.rt_bias[0:1, :], start=False, stop=True).then_inc(K.full(("rt", tt)), 1)
    for tt in range(TT):
        for hf in range(2):
            pe.wait_ge(K.empty(("h2", tt, hf)), K.empty_count(("h2", tt, hf)))
            bank = K.bank(("h2", tt, hf))
            for j in range(4):
                ins = pe.transpose(bank[:, j * P:(j + 1) * P], K.h2T[:, 4 * hf + j, tt * P:(tt + 1) * P], K.ident)
            ins.then_inc(K.full(("h2", tt, hf)), 1)
    gate_rows("g2", (10, 11))
    pe.wait_ge(K.sem["route"], K.count("route"))
    for tt in range(TT):
        pe.wait_ge(K.empty(("pos", tt)), K.empty_count(("pos", tt)))
        out = K.bank(("pos", tt))[:, 0:EXPERTS]
        if tt == 1:
            pe.matmul(out, K.ones, K.chosen[:, 0, :], start=True, stop=False)
        ins = pe.matmul(out, K.earlier, K.chosen[:, tt, :], start=tt == 0, stop=True)
        if tt == 1:
            total = K.bank(("pos", tt))[:, EXPERTS:2 * EXPERTS]
            pe.matmul(total, K.ones, K.chosen[:, 0, :], start=True, stop=False)
            ins = pe.matmul(total, K.ones, K.chosen[:, 1, :], start=False, stop=True)
        ins.then_inc(K.full(("pos", tt)), 1)


def tail_scalar(act, K):
    head_norm_scalar(act, K, ("yv",), "y_sq", "y_var", "y_std", "y_c")
    for tt in range(TT):
        act.wait_ge(K.sem["x3_var"], K.count("x3_var", 0, tt + 1))
        act.activation(K.x_std2[:, tt:tt + 1], K.x_mv2[:, tt, 1:2], ACT.Sqrt).then_inc(K.sem["x3_std"], 1)
    for tt in range(TT):
        act.wait_ge(K.sem["x4_var"], K.count("x4_var", 0, tt + 1))
        act.activation(K.x_std2[:, tt:tt + 1], K.x_mv2[:, tt, 1:2], ACT.Sqrt).then_inc(K.sem["x4_std"], 1)
    for q in range(4):
        act.wait_ge(K.full(("h2T", q)), K.full_count(("h2T", q)))
        bank = K.bank(("h2T", q))
        for j in range(2):
            kc = 2 * q + j
            ins = act.activation(K.h2T[:, kc, :], bank[:, j * T:(j + 1) * T], ACT.Identity,
                                 scale=K.mod[:, 1, DC + kc, 0:1], bias=K.mod[:, 1, kc, 0:1])
        ins.then_inc(K.empty(("h2T", q)), 1)
    for tt in range(TT):
        act.wait_ge(K.sem["rt_exp"], K.count("rt_exp", 0, tt + 1))
        act.activation(K.rt_t[:, tt, 0:GROUPS_E], K.rt_t[:, tt, 0:GROUPS_E], ACT.Exp, accum_out=K.rt_s[:, tt, 0:1])
        act.activation(K.rt_s[:, tt, 1:2], K.rt_s[:, tt, 1:2], ACT.Exp).then_inc(K.sem["rt_e2"], 1)
    for tt in range(TT):
        for hf in range(2):
            act.wait_ge(K.full(("h2", tt, hf)), K.full_count(("h2", tt, hf)))
            act.activation(K.x_hat[:, tt, hf * BANK:(hf + 1) * BANK], K.bank(("h2", tt, hf)), ACT.Copy).then_inc(
                K.empty(("h2", tt, hf)), 1)


def layer_norm_2(dve, K, link, name, row, signal_last):
    for tt in range(TT):
        dve.wait_ge(K.sem[name + "_std"], K.count(name + "_std", 0, tt + 1))
        x = K.x_tok[:, tt, :]
        dve.reciprocal(K.x_std2[:, tt:tt + 1], K.x_std2[:, tt:tt + 1]).then_inc(link.sem, 1)
        dve.wait_ge(link.sem, link.count())
        dve.tensor_scalar(x, x, K.x_mv2[:, tt, 0:1], K.x_std2[:, tt:tt + 1], ALU.subtract, ALU.mult).then_inc(link.sem, 1)
        dve.wait_ge(link.sem, link.count())
        dve.tensor_tensor(x, x, K.ln2_rows[:, row, :], ALU.mult).then_inc(link.sem, 1)
        dve.wait_ge(link.sem, link.count())
        ins = dve.tensor_tensor(x, x, K.ln2_rows[:, row + 1, :], ALU.add)
        if not signal_last or tt < TT - 1:
            ins.then_inc(link.sem, 1)
            dve.wait_ge(link.sem, link.count())
        else:
            ins.then_inc(K.sem[signal_last], 1)


def row_stats(dve, K, link, x, tt, name):
    for i in range(2):
        dve.bn_stats(K.bn3[:, i, :], x[:, i * BANK:(i + 1) * BANK]).then_inc(link.sem, 1)
        dve.wait_ge(link.sem, link.count())
    dve.bn_aggr(K.x_mv2[:, tt, :], K.bn3.rearrange("p a b -> p (a b)")).then_inc(link.sem, 1)
    dve.wait_ge(link.sem, link.count())
    dve.tensor_scalar(K.x_mv2[:, tt, 1:2], K.x_mv2[:, tt, 1:2], LN_EPS_2, None, ALU.add).then_inc(K.sem[name], 1)


def tail_vector(dve, K):
    link = Chain(K.dve_done, K.dve_base)
    tt_op, ts_op, stt = dve.tensor_tensor, dve.tensor_scalar, dve.scalar_tensor_tensor
    col = lambda name, i=0, n=1: K.vec2[:, VROWS[name][0] + i:VROWS[name][0] + i + n]
    for z in range(ZS):
        dve.wait_ge(K.empty(("lat", "y", z)), K.drained_count(("lat", "y", z), T // CH - 1))
        dve.wait_ge(K.empty(("lat", "s", z)), K.drained_count(("lat", "s", z), T // CH - 1))
    dve.sem_inc(K.sem["y_ready"], 4)
    dve.tensor_copy(K.c_rows, K.c_col[:, :, 0:1].broadcast_to([P, DC, P])).then_inc(K.sem["c_rows"], 1)
    head_norm_vector(dve, K, link, "ym", "yv", "y_c", "y_var", "y_std", K.y_sum, GN_EPS)
    for hp in range(HP):
        out = K.mixed[:, 4 + hp, :]
        ts_op(out, K.hn_c[:, hp, :], col("r_norm_w", hp), col("r_norm_b", hp), ALU.mult, ALU.add).then_inc(link.sem, 1)
        dve.wait_ge(link.sem, link.count())
        tt_op(out, out, K.bonus[:, hp, :], ALU.add).then_inc(link.sem, 1)
        dve.wait_ge(link.sem, link.count())
        tt_op(out, out, K.g_T[:, hp, :], ALU.mult).then_inc(K.sem["mixed_r"], 1)
    dve.wait_ge(K.sem["dma_tail"], K.count("dma_tail"))
    for i in range(2):
        part = slice(i * BANK, (i + 1) * BANK)
        dve.wait_ge(K.full(("g1", i)), K.full_count(("g1", i)))
        tt_op(K.g_rows[:, 0, part], K.bank(("g1", i)), K.g_bias[:, 0, part], ALU.add).then_inc(K.empty(("g1", i)), 1)
        dve.wait_ge(K.empty(("g1", i)), K.drained_count(("g1", i)))
    for tt in range(TT):
        for hf in range(2):
            part = slice(hf * BANK, (hf + 1) * BANK)
            x = K.x_tok[:, tt, part]
            dve.wait_ge(K.full(("out2", tt, hf)), K.full_count(("out2", tt, hf)))
            tt_op(K.tail_t, K.bank(("out2", tt, hf)), K.g_rows[:, 0, part], ALU.mult).then_inc(K.empty(("out2", tt, hf)), 1)
            dve.wait_ge(K.empty(("out2", tt, hf)), K.drained_count(("out2", tt, hf)))
            stt(out=x, in0=x, scalar=ALPHA_2, in1=K.tail_t, op0=ALU.mult, op1=ALU.add).then_inc(link.sem, 1)
            dve.wait_ge(link.sem, link.count())
        row_stats(dve, K, link, K.x_tok[:, tt, :], tt, "x3_var")
    layer_norm_2(dve, K, link, "x3", 0, None)
    for tt in range(TT):
        row_stats(dve, K, link, K.x_tok[:, tt, :], tt, "x4_var")
    for tt in range(TT):
        dve.wait_ge(K.sem["x4_std"], K.count("x4_std", 0, tt + 1))
        dve.reciprocal(K.x_std2[:, tt:tt + 1], K.x_std2[:, tt:tt + 1]).then_inc(link.sem, 1)
        dve.wait_ge(link.sem, link.count())
        ts_op(K.x_hat[:, tt, :], K.x_tok[:, tt, :], K.x_mv2[:, tt, 0:1], K.x_std2[:, tt:tt + 1], ALU.subtract, ALU.mult).then_inc(K.sem["x4"], 1)
    for tt in range(TT):
        route(dve, K, link, tt)
    for i in range(2):
        part = slice(i * BANK, (i + 1) * BANK)
        dve.wait_ge(K.full(("g2", i)), K.full_count(("g2", i)))
        tt_op(K.g_rows[:, 1, part], K.bank(("g2", i)), K.g_bias[:, 1, part], ALU.add).then_inc(K.empty(("g2", i)), 1)
        dve.wait_ge(K.empty(("g2", i)), K.drained_count(("g2", i)))
    plan(dve, K, link)
    dve.memset(K.acc, 0.0).then_inc(K.sem["acc_zero"], 1)
    dve.wait_ge(K.sem["acc_zero"], K.count("acc_zero"))
    K.dve_base = link.base + link.n


def route(dve, K, link, tt):
    tt_op, ts_op, stt = dve.tensor_tensor, dve.tensor_scalar, dve.scalar_tensor_tensor
    dve.wait_ge(K.full(("rt", tt)), K.full_count(("rt", tt)))
    bank = K.bank(("rt", tt))
    G, E = GROUPS_E, EXPERTS
    lg, le, t, s = K.rt_l[:, tt, 0:G], K.rt_l[:, tt, G:G + E], K.rt_t[:, tt, :], K.rt_s[:, tt, :]
    dve.tensor_copy(K.rt_l[:, tt, :], bank[:, 0:G + E]).then_inc(K.empty(("rt", tt)), 1)
    dve.wait_ge(K.empty(("rt", tt)), K.drained_count(("rt", tt)))

    def first_best(hot, values, n):
        dve.tensor_reduce(s[:, 2:3], values, AX_X, ALU.max).then_inc(link.sem, 1)
        dve.wait_ge(link.sem, link.count())
        stt(out=hot, in0=values, scalar=s[:, 2:3], in1=K.rank[:, 0:n], op0=ALU.is_equal, op1=ALU.mult).then_inc(link.sem, 1)
        dve.wait_ge(link.sem, link.count())
        dve.tensor_reduce(s[:, 3:4], hot, AX_X, ALU.max).then_inc(link.sem, 1)
        dve.wait_ge(link.sem, link.count())
        ts_op(hot, hot, s[:, 3:4], None, ALU.is_equal).then_inc(link.sem, 1)
        dve.wait_ge(link.sem, link.count())

    hot = K.rt_hot[:, tt, 0, 0:G]
    first_best(hot, lg, G)
    ts_op(t[:, 0:G], lg, s[:, 2:3], None, ALU.subtract).then_inc(link.sem, 1)
    dve.wait_ge(link.sem, link.count())
    eight = lambda a: a.rearrange("p (g e) -> p g e", g=G)
    wide = hot.unsqueeze(2).broadcast_to([P, G, PER_GROUP])
    tt_op(eight(le), eight(le), wide, ALU.mult).then_inc(link.sem, 1)
    dve.wait_ge(link.sem, link.count())
    ts_op(t[:, G:2 * G], hot, -1.0, BIG, ALU.add, ALU.mult).then_inc(link.sem, 1)
    dve.wait_ge(link.sem, link.count())
    tt_op(eight(le), eight(le), t[:, G:2 * G].unsqueeze(2).broadcast_to([P, G, PER_GROUP]), ALU.add).then_inc(link.sem, 1)
    dve.wait_ge(link.sem, link.count())
    hot1, hot2 = K.rt_hot[:, tt, 1, :], K.rt_hot[:, tt, 2, :]
    first_best(hot1, le, E)
    ts_op(s[:, 4:5], s[:, 2:3], 0.0, None, ALU.add).then_inc(link.sem, 1)
    dve.wait_ge(link.sem, link.count())
    stt(out=le, in0=hot1, scalar=-BIG, in1=le, op0=ALU.mult, op1=ALU.add).then_inc(link.sem, 1)
    dve.wait_ge(link.sem, link.count())
    first_best(hot2, le, E)
    tt_op(K.chosen[:, tt, :], hot1, hot2, ALU.add).then_inc(link.sem, 1)
    dve.wait_ge(link.sem, link.count())
    tt_op(s[:, 1:2], s[:, 2:3], s[:, 4:5], ALU.subtract).then_inc(K.sem["rt_exp"], 1)
    dve.wait_ge(K.sem["rt_e2"], K.count("rt_e2", 0, tt + 1))
    ts_op(s[:, 4:5], s[:, 1:2], 1.0, None, ALU.add).then_inc(link.sem, 1)
    dve.wait_ge(link.sem, link.count())
    tt_op(s[:, 4:5], s[:, 4:5], s[:, 0:1], ALU.mult).then_inc(link.sem, 1)
    dve.wait_ge(link.sem, link.count())
    dve.reciprocal(s[:, 4:5], s[:, 4:5]).then_inc(link.sem, 1)
    dve.wait_ge(link.sem, link.count())
    tt_op(s[:, 5:6], s[:, 4:5], s[:, 1:2], ALU.mult).then_inc(K.sem["route"], 1)
    dve.wait_ge(K.sem["route"], K.count("route", 0, tt + 1))


def plan(dve, K, link):
    tt_op, ts_op, stt = dve.tensor_tensor, dve.tensor_scalar, dve.scalar_tensor_tensor
    for tt in range(TT):
        dve.wait_ge(K.full(("pos", tt)), K.full_count(("pos", tt)))
    total = K.bank(("pos", 1))[:, EXPERTS:2 * EXPERTS]
    blocks, ends, first = (K.plan[:, k, :] for k in range(3))
    ts_op(blocks, total, 0.0, None, ALU.is_gt).then_inc(link.sem, 1)
    dve.wait_ge(link.sem, link.count())
    for k in range(1, T // PLACES):
        stt(out=blocks, in0=total, scalar=float(k * PLACES), in1=blocks, op0=ALU.is_gt, op1=ALU.add).then_inc(link.sem, 1)
        dve.wait_ge(link.sem, link.count())
    dve.tensor_tensor_scan(ends, K.ones[:, 0:EXPERTS], blocks, 0.0, ALU.mult, ALU.add).then_inc(link.sem, 1)
    dve.wait_ge(link.sem, link.count())
    tt_op(first, ends, blocks, ALU.subtract).then_inc(link.sem, 1)
    dve.wait_ge(link.sem, link.count())
    ts_op(first, first, float(PLACES), None, ALU.mult).then_inc(link.sem, 1)
    dve.wait_ge(link.sem, link.count())
    n = 2 * PAIRS
    tt_op(K.ended, K.token[:, 0:n].unsqueeze(2).broadcast_to([P, n, EXPERTS]), ends.unsqueeze(1).broadcast_to([P, n, EXPERTS]),
          ALU.is_ge).then_inc(link.sem, 1)
    dve.wait_ge(link.sem, link.count())
    dve.tensor_reduce(K.owner, K.ended, AX_X, ALU.add).then_inc(link.sem, 1)
    dve.wait_ge(link.sem, link.count())
    ts_op(K.owner, K.owner, float(EXPERTS - 1), None, ALU.min).then_inc(link.sem, 1)
    dve.wait_ge(link.sem, link.count())
    dve.tensor_copy(K.block_expert[:, 0:n], K.owner)
    dve.tensor_copy(K.block_expert[:, n:n + 1], ends[:, EXPERTS - 1:EXPERTS]).then_inc(K.sem["planned"], 1)
    for tt in range(TT):
        t = K.plan[:, 3, :]
        tt_op(K.chosen[:, tt, :], K.bank(("pos", tt))[:, 0:EXPERTS], first, ALU.add).then_inc(K.empty(("pos", tt)), 1)
        dve.wait_ge(K.empty(("pos", tt)), K.drained_count(("pos", tt)))
        for k in range(TOP):
            tt_op(t, K.chosen[:, tt, :], K.rt_hot[:, tt, 1 + k, :], ALU.mult).then_inc(link.sem, 1)
            dve.wait_ge(link.sem, link.count())
            dve.tensor_reduce(K.place[:, tt, k:k + 1], t, AX_X, ALU.add).then_inc(link.sem, 1)
            dve.wait_ge(link.sem, link.count())


def pair_sync(sp, K, A):
    sp.wait_ge(K.sem["planned"], K.count("planned"))
    blocks = block_count(sp, K)
    with sp.Fori(0, PAIRS) as i, sp.If(i * 2 < blocks):
        for j in range(2):
            e = sp.value_load(K.block_expert[0:1, bass.ds(i * 2 + j, 1)], min_val=0, max_val=EXPERTS - 1)
            for unit, a in (("pair_gate", A["ex_gate_2"]), ("pair_up", A["ex_up_2"]), ("pair_down", A["ex_down_2"])):
                sp.wait_ge(K.used_up((unit, j)), K.free_count((unit, j), i))
                sp.sem_inc(K.sync_steps, 1)
                weights = a[0, bass.ds(e, 1)].rearrange("a (k p) n -> p (a k) n", p=P)
                sp.dma_start(K.slot_like((unit, j), weights), weights).then_inc(K.landed((unit, j)), 16)


def block_count(eng, K):
    eng.wait_ge(K.sem["planned"], K.count("planned"))
    return eng.value_load(K.block_expert[0:1, 2 * PAIRS:2 * PAIRS + 1], min_val=1, max_val=BLOCKS)


def select(dve, K, link):
    tt_op, ts_op, stt = dve.tensor_tensor, dve.tensor_scalar, dve.scalar_tensor_tensor
    slots = K.token[:, 0:2 * PLACES]
    for tt in range(TT):
        one, two = K.place[:, tt, 0:1], K.place[:, tt, 1:2]
        ts_op(K.hit[:, tt, 0, :], slots, one, None, ALU.is_equal)
        ts_op(K.hit[:, tt, 1, :], slots, one, K.rt_s[:, tt, 4:5], ALU.is_equal, ALU.mult)
        ts_op(K.hit[:, tt, 2, :], slots, two, K.rt_s[:, tt, 5:6], ALU.is_equal, ALU.mult).then_inc(link.sem, 1)
    dve.wait_ge(link.sem, link.count() + 1)
    link.count()
    for tt in range(TT):
        stt(out=K.chosen_at[:, tt, :], in0=slots, scalar=K.place[:, tt, 1:2], in1=K.hit[:, tt, 0, :], op0=ALU.is_equal, op1=ALU.add)
        ins = tt_op(K.weight_at[:, tt, :], K.hit[:, tt, 1, :], K.hit[:, tt, 2, :], ALU.add)
    ins.then_inc(K.sem["selected"], 1)


def pair_tensor(pe, K):
    for tt in range(TT):
        for hf in range(2):
            pe.wait_ge(K.empty(("h2", tt, hf)), K.drained_count(("h2", tt, hf)))
    blocks = block_count(pe, K)
    with pe.Fori(0, PAIRS) as i, pe.If(i * 2 < blocks):
        pe.wait_ge(K.sem["selected"], K.count("selected", i))
        for q in range(2):
            pe.wait_ge(K.empty(("xg", q)), K.empty_count(("xg", q), i))
            bank = K.bank(("xg", q))
            for u in range(4):
                kc = 4 * q + u
                for tt in range(TT):
                    ins = pe.matmul(bank[:, u * P:(u + 1) * P], K.x_hat[:, tt, kc * P:(kc + 1) * P], K.chosen_at[:, tt, :],
                                    start=tt == 0, stop=tt == TT - 1)
            ins.then_inc(K.full(("xg", q)), 1)
        for j in range(2):
            mine = slice(j * PLACES, (j + 1) * PLACES)
            for name, unit in (("pgate", "pair_gate"), ("pup", "pair_up")):
                pe.wait_ge(K.landed((unit, j)), K.landed_count((unit, j), i))
                w = K.weights((unit, j), DC, D_EXPERT)
                pe.wait_ge(K.empty((name, j)), K.empty_count((name, j), i))
                bank = K.bank((name, j))
                for c in range(EC):
                    for kc in range(DC):
                        if j == 0 and name == "pgate" and c == 0 and kc % 4 == 0:
                            pe.wait_ge(K.empty(("xg", kc // 4)), K.drained_count(("xg", kc // 4), i))
                        ins = pe.matmul(bank[:, c * PLACES:(c + 1) * PLACES], w[:, kc, c * P:(c + 1) * P], K.xg[:, kc, mine],
                                        start=kc == 0, stop=kc == DC - 1)
                ins.then_inc(K.full((name, j)), 1)
            if j == 0:
                pe.wait_ge(K.empty(("putT", 0)), K.empty_count(("putT", 0), i))
                for tt in range(TT):
                    ins = pe.transpose(K.bank(("putT", 0))[:, tt * P:(tt + 1) * P], K.weight_at[:, tt, :], K.ident)
                ins.then_inc(K.full(("putT", 0)), 1)
            pe.wait_ge(K.landed(("pair_down", j)), K.landed_count(("pair_down", j), i))
            w = K.weights(("pair_down", j), EC, D)
            pe.wait_ge(K.empty(("pup", j)), K.drained_count(("pup", j), i))
            for hf in range(2):
                if j == 0:
                    pe.wait_ge(K.empty(("pdown", hf)), K.empty_count(("pdown", hf), i))
                for kc in range(EC):
                    ins = pe.matmul(K.bank(("pdown", hf))[mine, :], K.p_hid[:, j, kc, :], w[:, kc, hf * BANK:(hf + 1) * BANK],
                                    start=kc == 0, stop=kc == EC - 1)
                if j == 1:
                    ins.then_inc(K.full(("pdown", hf)), 1)
                elif hf == 1:
                    ins.then_inc(K.used_up(("pair_down", j)), 1)
        pe.wait_ge(K.empty(("putT", 0)), K.drained_count(("putT", 0), i))
        for hf in range(2):
            pe.wait_ge(K.empty(("pdown", hf)), K.drained_count(("pdown", hf), i))
            for tt in range(TT):
                pe.wait_ge(K.empty(("put", tt, hf)), K.empty_count(("put", tt, hf), i))
                pe.matmul(K.bank(("put", tt, hf)), K.put_T[:, tt, :], K.p_out[:, hf, :], start=True, stop=True).then_inc(
                    K.full(("put", tt, hf)), 1)


def pair_scalar(act, K):
    blocks = block_count(act, K)
    with act.Fori(0, PAIRS) as i, act.If(i * 2 < blocks):
        for q in range(2):
            act.wait_ge(K.full(("xg", q)), K.full_count(("xg", q), i))
            act.activation(K.xg[:, 4 * q:4 * q + 4, :], by_pair(K.bank(("xg", q))), ACT.Copy).then_inc(K.empty(("xg", q)), 1)
        for j in range(2):
            act.wait_ge(K.empty(("pup", j)), K.drained_count(("pup", j), i, ago=1))
            act.wait_ge(K.full(("pgate", j)), K.full_count(("pgate", j), i))
            act.activation(K.p_silu[:, j, :], K.bank(("pgate", j))[:, 0:EC * PLACES], ACT.Silu).then_inc(K.empty(("pgate", j)), 1)
            if j == 0:
                act.wait_ge(K.full(("putT", 0)), K.full_count(("putT", 0), i))
                act.activation(K.put_T.rearrange("p a b -> p (a b)"), K.bank(("putT", 0))[:, 0:T], ACT.Copy).then_inc(
                    K.empty(("putT", 0)), 1)
        for hf in range(2):
            act.wait_ge(K.full(("pdown", hf)), K.full_count(("pdown", hf), i))
            act.activation(K.p_out[:, hf, :], K.bank(("pdown", hf)), ACT.Copy).then_inc(K.empty(("pdown", hf)), 1)


def pair_vector(dve, K):
    blocks = block_count(dve, K)
    link = Chain(K.place_done)
    select(dve, K, link)
    with dve.Fori(0, PAIRS) as i, dve.If(i * 2 < blocks):
        link = Chain(K.place_done, SELECT_STEPS, i, SELECT_STEPS + 2)
        for j in range(2):
            dve.wait_ge(K.empty(("pgate", j)), K.drained_count(("pgate", j), i))
            dve.wait_ge(K.full(("pup", j)), K.full_count(("pup", j), i))
            dve.tensor_tensor(K.p_hid[:, j].rearrange("p k n -> p (k n)"), K.p_silu[:, j, :],
                              K.bank(("pup", j))[:, 0:EC * PLACES], ALU.mult).then_inc(K.empty(("pup", j)), 1)
            if j == 0:
                dve.wait_ge(K.full(("putT", 0)), K.full_count(("putT", 0), i))
                dve.wait_ge(K.sem["selected"], K.count("selected", i))
                dve.tensor_scalar(K.place, K.place, 2.0 * PLACES, None, ALU.subtract).then_inc(link.sem, 1)
                dve.wait_ge(link.sem, link.count())
                select(dve, K, link)
        for hf in range(2):
            for tt in range(TT):
                key = ("put", tt, hf)
                part = K.acc[:, tt, hf * BANK:(hf + 1) * BANK]
                dve.wait_ge(K.empty(key), K.drained_count(key, i, ago=1))
                dve.wait_ge(K.full(key), K.full_count(key, i))
                dve.tensor_tensor(part, part, K.bank(key), ALU.add).then_inc(K.empty(key), 1)
        for hf in range(2):
            for tt in range(TT):
                dve.wait_ge(K.empty(("put", tt, hf)), K.drained_count(("put", tt, hf), i))
        dve.sem_inc(link.sem, 1)
        link.count()


def finish_vector(dve, K):
    link = Chain(K.dve_done, K.dve_base)
    for tt in range(TT):
        dve.tensor_tensor(K.acc[:, tt, :], K.acc[:, tt, :], K.g_rows[:, 1, :], ALU.mult).then_inc(link.sem, 1)
        dve.wait_ge(link.sem, link.count())
        x = K.x_tok[:, tt, :]
        dve.scalar_tensor_tensor(out=x, in0=x, scalar=ALPHA_2, in1=K.acc[:, tt, :], op0=ALU.mult, op1=ALU.add).then_inc(link.sem, 1)
        dve.wait_ge(link.sem, link.count())
        row_stats(dve, K, link, x, tt, "x5_var")
    layer_norm_2(dve, K, link, "x5", 2, "x5")


def finish_scalar(act, K):
    for tt in range(TT):
        act.wait_ge(K.sem["x5_var"], K.count("x5_var", 0, tt + 1))
        act.activation(K.x_std2[:, tt:tt + 1], K.x_mv2[:, tt, 1:2], ACT.Sqrt).then_inc(K.sem["x5_std"], 1)


NAMES = ["x", "w_in", "sgu_ln_g", "sgu_ln_b", "sgu_w", "sgu_b", "ssm_lambda_re", "ssm_lambda_im", "ssm_log_dt",
         "ssm_b_re", "ssm_b_im", "ssm_c_re", "ssm_c_im", "ssm_d", "glu_w", "glu_b", "w_branch_a", "w_branch_b",
         "w_branch_c", "w_out", "ln1_g", "ln1_b", "ffn_w1", "ffn_w3", "ffn_w2", "ln2_g", "ln2_b", "c_2", "ctx_2",
         "c_ctx_2", "w_ada_2", "b_ada_2", "w_in_2", "conv_w_2", "m_bias_i_2", "m_bias_f_2", "m_norm_w_2", "r_w0_2",
         "r_wB_2", "r_a0_2", "r_aB_2", "r_gB_2", "r_kk_2", "r_ka_2", "r_bonus_2", "r_norm_w_2", "r_norm_b_2", "w_out_2",
         "ln1_g_2", "ln1_b_2", "ln2_g_2", "ln2_b_2", "rt_g_2", "rt_g_b_2", "rt_e_2", "rt_e_b_2", "ex_gate_2", "ex_up_2",
         "ex_down_2"]


class Arena:

    def __init__(self, sbuf, size):
        self.sbuf, self.size, self.at, self.top = sbuf, size, 0, 0

    def __call__(self, *shape):
        n = int(np.prod(shape))
        view = self.sbuf[:, self.at:self.at + n]
        self.at += n
        self.top = max(self.top, self.at)
        assert self.at <= self.size, f"{self.at} of {self.size}"
        names = "abc"[:len(shape)]
        if len(shape) > 1:
            view = view.rearrange(f"p ({' '.join(names)}) -> p {' '.join(names)}", **dict(zip(names, shape)))
        return view


ARENA = 40856


def layer_tiles(K, tile):
    K.x_tok, K.xT = tile(TT, D), tile(DC, T)
    K.uT, K.v_ln, K.zssm, K.y_g, K.oT, K.av = (tile(WC, T) for _ in range(6))
    K.v_ln = K.v_ln.rearrange("p a b -> p (a b)").rearrange("p (a b) -> p a b", a=TT)
    K.av = K.av.rearrange("p a b -> p (a b)").rearrange("p (a b) -> p a b", a=TT)
    at = tile.at
    K.qT, K.kT = tile(WC, T), tile(WC, T)
    tile.at = at
    K.merged = tile(DC, T)
    at = tile.at
    K.hT = tile(FC, T)
    tile.at = at
    K.gates = tile(3 * DC, T)
    K.bT_re, K.bT_im = tile(4, BANK), tile(4, BANK)
    K.cT_re, K.cT_im = tile(WC, P), tile(WC, P)
    K.b_nat_re, K.b_nat_im = tile(ST, 32), tile(ST, 32)
    K.c_nat_re, K.c_nat_im = tile(WC, P), tile(WC, P)
    K.w_nat, K.wT = tile(WC, P), tile(WC, P)
    K.vrows, K.vec, K.dtrow, K.sgu_bias = tile(P), tile(P), tile(2), tile(W5)
    K.v_gain, K.v_bias = (K.oT.rearrange("p a b -> p (a b)")[:, i * W5:(i + 1) * W5] for i in range(2))
    K.sv, K.decay = tile(11, ST), tile(ST)
    K.v_mv, K.v_std, K.x_mv, K.x_std, K.bn = tile(TT, 2), tile(TT), tile(TT, 2), tile(TT), tile(2, 6)
    K.score, K.prob, K.probT = tile(2, 3 * P), tile(2, 3 * P), tile(2, 3 * P)
    K.negmax, K.rowsum = tile(2, 2), tile(2, 2)
    K.dve_tmp = tile(4, BANK)
    K.silu = K.dve_tmp[:, 2:4, :]
    at = tile.at
    K.ln_rows = tile(4, D)
    tile.at = at
    K.cos, K.sin, K.g_re, K.g_im = (tile(2, BANK) for _ in range(4))
    K.h_re, K.h_im = tile(2, BANK), tile(2, BANK)
    K.bbar_re, K.bbar_im = (h.rearrange("p a b -> p (a b)")[:, 0:ST * 32].rearrange("p (a b) -> p a b", a=ST)
                            for h in (K.h_re, K.h_im))
    K.angle, K.pool_tmp = tile(BANK), tile(2, BANK)


class Step:

    def __init__(self, tile):
        self.p, self.p_inv, self.kr = tile(HP, CH + 1), tile(HP, CH), tile(HP, P + CH)
        self.b, self.k, self.v, self.z, self.zt, self.inv, self.nt = (tile(HP, P) for _ in range(7))
        self.rb, self.rk = tile(HP, CH), tile(HP, CH)
        self.bt, self.kt, self.vt, self.a1, self.u, self.s = (tile(HP, P) for _ in range(6))


def flat(a):
    return a.rearrange("p a b -> p (a b)")


def split(a, n):
    return a.rearrange("p (a b) -> p a b", a=n)


def second_tiles(K, tile):
    K.head_ones, K.head_mean, K.neg_mask, K.upto_mask, K.vec2 = tile(P), tile(P), tile(ZS, P), tile(ZS, CH), tile(P)
    K.c_col, K.mod, K.rt_bias, K.rank = tile(DC, 2), tile(2, 2 * DC, 2), tile(GROUPS_E + EXPERTS), tile(EXPERTS)
    K.nrm_mv, K.nrm_std, K.bn2, K.bn3 = tile(2 * TT, 2), tile(2, TT), tile(2, 6), tile(2, 6)
    K.nrm_mv = K.nrm_mv.rearrange("p (s a) b -> p s a b", s=2)
    K.x_mv2, K.x_std2 = tile(TT, 2), tile(TT)
    K.rt_l, K.rt_t, K.rt_s = tile(TT, GROUPS_E + EXPERTS), tile(TT, 2 * GROUPS_E), tile(TT, 6)
    K.rt_hot = tile(TT, 3 * EXPERTS).rearrange("p t (k e) -> p t k e", k=3)
    K.earlier = tile(P)
    K.r_T, K.g_T, K.bonus, K.y_sum, K.mixed = tile(HP, T), tile(HP, T), tile(HP, T), tile(HP, T), tile(DC, T)
    dead = tile.at
    K.kmod, K.rv, K.aT, K.kh = (tile(HP, S_ALL) for _ in range(4))
    cum = tile.at
    K.cum = tile(ZS * HP, S_ALL).rearrange("p (z c) t -> p z c t", z=ZS)
    rest = tile.at
    tile.at = dead
    K.ln2_rows, K.g_bias, K.g_rows, K.x_hat, K.h2T = tile(4, D), tile(2, D), tile(2, D), tile(TT, D), tile(DC, T)
    assert tile.at <= rest
    tile.at = cum
    K.nrm = tile(2 * TT, D).rearrange("p (s a) d -> p s a d", s=2)
    K.ss_root, K.sw, K.bonus_in = split(flat(K.y_sum), 2), split(flat(K.mixed[:, 0:4, :]), 2), split(flat(K.mixed[:, 4:, :]), 2)

    tile.at = rest
    rows = tile(6, BANK)
    K.li_row, K.lf_row, K.row_t, K.b_row, K.G_row, K.g_row = (rows[:, i, :] for i in range(6))
    K.guard, K.den_abs = K.li_row, K.lf_row
    K.hn_c, K.hn_sq = split(flat(rows[:, 2:4, :]), HP), split(K.G_row, 2)
    K.tmp2 = tile(1, BANK)
    K.hn_v = split(K.tmp2[:, 0, :], 2)
    tail = tile.at
    K.hsT = tile(DC, S_ALL)
    K.st = K.hsT.rearrange("p (h z s) (a t) -> p h z (s a) t", h=2, z=ZS, a=2)
    K.qm, K.km, lora = tile(HP, T), tile(HP, S_ALL), tile(4, BANK)
    K.wB, K.aB, K.gB, K.lwT = (lora[:, i, :] for i in range(4))
    K.mv = lora
    K.laT, K.lgT, K.sq = tile(BANK), tile(T), tile(2, BANK)
    K.mixed_gate = split(flat(K.sq), HP)
    K.neg_G, K.neg_m = tile(T), tile(T)
    pick = tile(ZS * HH, P)
    K.pick = pick.rearrange("p (z h) n -> p z h n", z=ZS)
    K.go_on = split(flat(pick[:, 0:ZS * S_ALL // P, :]), ZS)
    K.gate_w = pick[:, ZS * S_ALL // P:, :]
    assert ZS * S_ALL // P + DC <= ZS * HH
    K.g_col, K.taps, K.vrows2, K.crows = tile(SB, Z0 + HH), tile(9, CONV_CHUNKS), tile(P), tile(2, P)
    K.bias_i, K.bias_f = tile(1), tile(1)
    tile.at = rest
    K.step = [Step(tile) for _ in range(ZS)]
    tile.at = tail
    K.c_rows, K.rt_w, K.tail_t = tile(DC, P), tile(DC, GROUPS_E + EXPERTS), tile(BANK)
    K.acc = tile(TT, D)
    K.chosen_at, K.weight_at, K.put_T, K.xg = tile(TT, P), tile(TT, P), tile(TT, P), tile(DC, P)
    K.p_silu, K.p_hid, K.p_out = tile(2, EC * PLACES), tile(2 * EC, PLACES), tile(2, BANK)
    K.p_hid = K.p_hid.rearrange("p (j k) n -> p j k n", j=2)
    K.hit = tile(3 * TT, P).rearrange("p (t k) n -> p t k n", t=TT)
    K.ended, K.owner = tile(2 * PAIRS, EXPERTS), tile(2 * PAIRS)
    K.chosen, K.plan, K.place = tile(TT, EXPERTS), tile(4, EXPERTS), tile(TT, TOP)


def constants(pool, K):
    link = Chain(K.setup_done)
    pool.memset(K.ident, 0.0).then_inc(link.sem, 1)
    pool.wait_ge(link.sem, link.count())
    pool.affine_select(out=K.ident, in_=K.ident, compare_op=ALU.not_equal, fill=1.0, base=0,
                            pattern=[[-1, P]], channel_multiplier=1).then_inc(link.sem, 1)
    pool.wait_ge(link.sem, link.count())
    pool.iota(K.token, pattern=[[1, T]], base=0, channel_multiplier=0, allow_small_or_imprecise_dtypes=True).then_inc(link.sem, 1)
    pool.wait_ge(link.sem, link.count())
    for lo, n, base in ((0, P, 0), (P, T, -P)):
        part = K.distance[:, lo:lo + n]
        pool.iota(part, pattern=[[1, n]], base=base, channel_multiplier=-1, allow_small_or_imprecise_dtypes=True).then_inc(link.sem, 1)
        pool.wait_ge(link.sem, link.count())
        pool.affine_select(out=part, in_=part, compare_op=ALU.is_ge, fill=MASKED, base=-base,
                                pattern=[[-1, n]], channel_multiplier=1).then_inc(link.sem, 1)
        pool.wait_ge(link.sem, link.count())
    for tile, value in ((K.ones, 1.0), (K.half_pi, math.pi / 2), (K.vrows, 0.0), (K.bT_re, 0.0), (K.bT_im, 0.0),
                        (K.b_nat_re, 0.0), (K.b_nat_im, 0.0), (K.c_nat_re, 0.0), (K.c_nat_im, 0.0)):
        pool.memset(tile, value).then_inc(link.sem, 1)
        pool.wait_ge(link.sem, link.count())
    for credit in K.bank_drained + K.slot_used:
        pool.sem_inc(credit, 1)
    pool.sem_inc(K.sem["params_free"], 1)
    pool.sem_inc(K.ready, 1)


SELECT_STEPS = 2
DVE_LINKS, ACT_LINKS, POOL_LINKS = 123, 8, 67


def program(nc, A, out):
    phases = [Phase("layers", DEPTH, layer_groups(), layer_units(), layer_closes()),
              Phase("mid", 1, mid_groups(), mid_units(), mid_closes()),
              Phase("ctx", T // CH, chunk_groups("ctx", False), [], {}),
              Phase("lat", T // CH, chunk_groups("lat", True), [], {}),
              Phase("tail", 1, tail_groups(), tail_units(), tail_closes()),
              Phase("pairs", PAIRS, pair_groups(), pair_units(), pair_closes())]
    with ExitStack() as ctx:
        sem = lambda name: ctx.enter_context(nc.semaphore(name))
        K = Kit(nc, ctx, phases, LAYER_EVENTS | MID_EVENTS | CHUNK_EVENTS | TAIL_EVENTS)
        K.setup_done, K.dve_done, K.act_done, K.pool_done = map(sem, ("setup_done", "dve_done", "act_done", "pool_done"))
        K.ready, K.dma_x, K.dma_out, K.place_done = map(sem, ("ready", "dma_x", "dma_out", "place_done"))
        K.dve_links = DVE_LINKS
        K.dve_base, K.act_base, K.pool_base = DEPTH * DVE_LINKS, DEPTH * ACT_LINKS, DEPTH * POOL_LINKS
        K.block_expert = ctx.enter_context(nc.sbuf_tensor("block_expert", [P, 2 * PAIRS + 1], mybir.dt.int32))
        sbuf = ctx.enter_context(nc.sbuf_tensor("arena", [P, ARENA], F32))
        tile = Arena(sbuf, ARENA)
        K.ident, K.token, K.distance, K.ones, K.half_pi = tile(P), tile(T), tile(3 * P), tile(P), tile(1)
        after_x = tile.at + TT * D
        layer_tiles(K, tile)
        tile.at = after_x
        second_tiles(K, tile)

        block = ctx.enter_context(nc.Block())

        @block.sync
        def _(sp):
            sp.dma_start(K.x_tok, A["x"][0].rearrange("(a p) d -> p a d", p=P)).then_inc(K.dma_x, 16)
            sp.wait_ge(K.ready, 1)
            layer_sync(sp, K, A)
            mid_sync(sp, K, A)
            tail_sync(sp, K, A)
            pair_sync(sp, K, A)
            sp.wait_ge(K.sem["x5"], K.count("x5"))
            sp.dma_start(out[0].rearrange("(a p) d -> p a d", p=P), K.x_tok).then_inc(K.dma_out, 16)
            sp.wait_ge(K.dma_out, 16)

        @block.gpsimd
        def _(pool):
            constants(pool, K)
            layer_gpsimd(pool, K)
            mid_gpsimd(pool, K)
            chunk_tiles_gpsimd(pool, K)
            chunk_gpsimd(pool, K, "ctx", False)
            chunk_gpsimd(pool, K, "lat", True)

        @block.scalar
        def _(act):
            act.wait_ge(K.ready, 1)
            layer_scalar(act, K)
            mid_scalar(act, K)
            chunk_scalar(act, K, "ctx", False)
            chunk_scalar(act, K, "lat", True)
            tail_scalar(act, K)
            pair_scalar(act, K)
            finish_scalar(act, K)

        @block.tensor
        def _(pe):
            pe.wait_ge(K.ready, 1)
            layer_tensor(pe, K)
            mid_tensor(pe, K)
            chunk_tensor(pe, K, "ctx", False)
            chunk_tensor(pe, K, "lat", True)
            tail_tensor(pe, K)
            pair_tensor(pe, K)

        @block.vector
        def _(dve):
            dve.wait_ge(K.ready, 1)
            dve.wait_ge(K.dma_x, 16)
            dve.sem_inc(K.sem["x_in"], 1)
            layer_vector(dve, K)
            mid_vector(dve, K)
            chunk_vector(dve, K, "ctx", False)
            chunk_vector(dve, K, "lat", True)
            tail_vector(dve, K)
            pair_vector(dve, K)
            finish_vector(dve, K)


def kernel(**inputs):
    import numpy as _np
    import concourse.bacc as _bacc
    from concourse import mybir as _mybir
    from concourse.bass_utils import run_bass_kernel_spmd as _run

    nc = _bacc.Bacc("TRN2", target_bir_lowering=False, num_devices=1)
    arrays, args = {}, {}
    for name in NAMES:
        a = _np.ascontiguousarray(inputs[name])
        arrays[f"in_{name}_dram"] = a
        args[name] = nc.dram_tensor(f"in_{name}_dram", a.shape, _mybir.dt.from_np(a.dtype), kind="ExternalInput").ap()
    out = nc.dram_tensor("out_0_dram", (1, T, D), F32, kind="ExternalOutput").ap()
    program(nc, args, out)
    r = _run(nc, [arrays], core_ids=[0])
    return r.results[0]["out_0_dram"]
```
